# Optimizing a Trainium2 kernel written in Bass

```python
import jax, jax.numpy as jnp
from jax import lax
import numpy as np

D_MODEL = 4096
BATCH = 1
SEQ = 256
DEPTH = 1

HGRN_HEADS = 16
HGRN_KEY_DIM = 128
HGRN_VAL_DIM = 128
HGRN_KEY_WIDTH = HGRN_HEADS * HGRN_KEY_DIM
HGRN_VAL_WIDTH = HGRN_HEADS * HGRN_VAL_DIM
CHUNK = 64
CONV_WIDTH = 2048
CONV_GROUPS = 16
CONV_K = 3
SPLIT_SIZES = (
    HGRN_KEY_WIDTH,
    HGRN_KEY_WIDTH,
    HGRN_VAL_WIDTH,
    HGRN_VAL_WIDTH,
    CONV_WIDTH,
    CONV_WIDTH,
    CONV_WIDTH,
    CONV_WIDTH,
    D_MODEL,
    D_MODEL,
)
IN_COLS = sum(SPLIT_SIZES)
EPS = 1e-6

kernel_name = "hgrn2_shortconv_gated_hybrid"

def rmsnorm(x, w):
    xf = x.astype(jnp.float32)
    y = xf * lax.rsqrt(jnp.mean(xf * xf, axis=-1, keepdims=True) + EPS)
    return (y * w.astype(jnp.float32)).astype(x.dtype)

def hgrn2_chunkwise(q, log_f, k, v):
    bsz, t_len, n_heads, dk = q.shape
    dv = v.shape[-1]
    n_chunks = t_len // CHUNK

    def to_chunks(a):
        return a.reshape(bsz, n_chunks, CHUNK, n_heads, a.shape[-1]).transpose(1, 0, 3, 2, 4)

    causal = jnp.tril(jnp.ones((CHUNK, CHUNK), dtype=bool))[:, :, None]

    def step(state, inp):
        qc, gc, kc, vc = inp
        b = jnp.cumsum(gc, axis=2)
        o_inter = jnp.einsum('bhtd,bhde->bhte', qc * jnp.exp(b), state)
        diff = b[:, :, :, None, :] - b[:, :, None, :, :]
        decay = jnp.exp(jnp.where(causal, diff, -jnp.inf))
        scores = jnp.einsum('bhtd,bhsd,bhtsd->bhts', qc, kc, decay)
        o_intra = jnp.einsum('bhts,bhse->bhte', scores, vc)
        b_last = b[:, :, -1:, :]
        state = (jnp.exp(b_last[:, :, 0, :])[..., None] * state
                 + jnp.einsum('bhsd,bhse->bhde', kc * jnp.exp(b_last - b), vc))
        return state, o_inter + o_intra

    s0 = jnp.zeros((bsz, n_heads, dk, dv), jnp.float32)
    _, o = lax.scan(step, s0, (to_chunks(q), to_chunks(log_f), to_chunks(k), to_chunks(v)))
    return o.transpose(1, 0, 3, 2, 4).reshape(bsz, t_len, n_heads, dv)

def causal_depthwise_conv(u, w):
    rhs = w.reshape(CONV_K, 1, u.shape[-1]).astype(u.dtype)
    return lax.conv_general_dilated(
        u, rhs, window_strides=(1,), padding=[(CONV_K - 1, 0)],
        dimension_numbers=('NWC', 'WIO', 'NWC'), feature_group_count=u.shape[-1])

def setup_inputs(seed: int = 0) -> dict:
    key = jax.random.key(seed)
    ks = jax.random.split(key, 12)
    f32 = jnp.float32
    x = jax.random.normal(ks[0], (BATCH, SEQ, D_MODEL), f32)
    norm_w = 1.0 + 0.02 * jax.random.normal(ks[1], (DEPTH, D_MODEL), f32)
    w_in = jax.random.normal(ks[2], (DEPTH, D_MODEL, IN_COLS), f32) * D_MODEL ** -0.5
    lb_logits = 0.5 * jax.random.normal(ks[3], (DEPTH + 1, HGRN_KEY_WIDTH), f32)
    hgrn_norm_w = 1.0 + 0.02 * jax.random.normal(ks[4], (DEPTH, HGRN_VAL_DIM), f32)
    conv_w = jax.random.normal(ks[5], (DEPTH, CONV_K, CONV_WIDTH), f32) * CONV_K ** -0.5
    w_branch_a = jax.random.normal(ks[6], (DEPTH, HGRN_VAL_WIDTH, D_MODEL), f32) * HGRN_VAL_WIDTH ** -0.5
    w_branch_b = jax.random.normal(ks[7], (DEPTH, CONV_WIDTH, D_MODEL), f32) * CONV_WIDTH ** -0.5
    gate_bias = 0.01 * jax.random.normal(ks[8], (DEPTH, 2, D_MODEL), f32)
    w_out = jax.random.normal(ks[9], (DEPTH, D_MODEL, D_MODEL), f32) * D_MODEL ** -0.5
    final_norm_w = 1.0 + 0.02 * jax.random.normal(ks[10], (D_MODEL,), f32)
    return {"x": x, "norm_w": norm_w, "w_in": w_in, "lb_logits": lb_logits,
            "hgrn_norm_w": hgrn_norm_w, "conv_w": conv_w, "w_branch_a": w_branch_a,
            "w_branch_b": w_branch_b, "gate_bias": gate_bias, "w_out": w_out,
            "final_norm_w": final_norm_w}

def reference(x, norm_w, w_in, lb_logits, hgrn_norm_w, conv_w, w_branch_a,
              w_branch_b, gate_bias, w_out, final_norm_w):
    bsz, t_len, _ = x.shape
    f32 = jnp.float32
    lower_bounds = jnp.cumsum(jax.nn.softmax(lb_logits.astype(f32), axis=0), axis=0)
    split_points = list(np.cumsum(SPLIT_SIZES)[:-1])
    h = x
    for layer in range(DEPTH):
        u = rmsnorm(h, norm_w[layer])
        proj = jnp.einsum('btd,dc->btc', u, w_in[layer])
        (a_q, a_f, a_i, a_g, c_b, c_c, c_h, c_g, g_a, g_b) = jnp.split(proj, split_points, axis=-1)

        lb = lower_bounds[layer]
        f = lb + (1.0 - lb) * jax.nn.sigmoid(a_f.astype(f32))
        log_f = jnp.log(f)
        k = 1.0 - f
        hs = (bsz, t_len, HGRN_HEADS)
        o_a = hgrn2_chunkwise(a_q.astype(f32).reshape(hs + (HGRN_KEY_DIM,)),
                              log_f.reshape(hs + (HGRN_KEY_DIM,)),
                              k.reshape(hs + (HGRN_KEY_DIM,)),
                              a_i.astype(f32).reshape(hs + (HGRN_VAL_DIM,)))
        o_a = rmsnorm(o_a, hgrn_norm_w[layer]).reshape(bsz, t_len, HGRN_VAL_WIDTH).astype(x.dtype)
        y_a = o_a * jax.nn.silu(a_g)

        conv = causal_depthwise_conv(c_c * c_h, conv_w[layer])
        y_b = (c_b * conv) * jax.nn.silu(c_g)

        z_a = jnp.einsum('btc,cd->btd', y_a, w_branch_a[layer])
        z_b = jnp.einsum('btc,cd->btd', y_b, w_branch_b[layer])
        merged = (jax.nn.sigmoid(g_a + gate_bias[layer, 0]) * z_a
                  + jax.nn.sigmoid(g_b + gate_bias[layer, 1]) * z_b)
        h = h + jnp.einsum('btd,de->bte', merged, w_out[layer])
    return rmsnorm(h, final_norm_w)


_drawn_inputs = setup_inputs


def setup_inputs(seed=0):
    import zlib

    import numpy as np

    out = dict(_drawn_inputs(seed))
    spreads = {}
    factors = {'norm_w': 3.142, 'hgrn_norm_w': 64.0, 'gate_bias': 25.331, 'final_norm_w': 8.137}
    for name, (base, spread) in spreads.items():
        noise = np.random.default_rng([zlib.crc32(name.encode()), seed]).standard_normal(out[name].shape)
        drawn = base * np.exp(spread * noise) if base else spread * noise
        out[name] = __import__('jax').numpy.asarray(drawn.astype(out[name].dtype))
    for name, factor in factors.items():
        out[name] = (out[name] * factor).astype(out[name].dtype)
    return out
```

```python
import concourse.bass as bass
from concourse import mybir
from contextlib import ExitStack

F32 = mybir.dt.float32
F32R = mybir.dt.float32r
U32 = mybir.dt.uint32
ALU = mybir.AluOpType
ACT = mybir.ActivationFunctionType
AX = mybir.AxisListType

P = 128
T = 256
D = 4096
KT = D // P
BW = 2048
KB = BW // P
GW = 256
KC = 4
RING = 4
CD, CB = KT // KC, KB // KC
NP = BW // GW
NG = D // GW
SLOTS = 16
LEVELS = (1, 2, 4, 8, 16, 32, 64, 128)
EPS = 1e-6
A_Q, A_F, A_I, A_G, C_B, C_C, C_H, C_G = (BW * n for n in range(8))
G_A, G_B = 8 * BW, 8 * BW + D
HGRN_GROUPS = (A_F, A_Q, A_I, A_G)
CONV_GROUPS = (C_G, C_C, C_H, C_B)
TURNS_BRANCH = 4 * CD // RING
TURNS_MERGE = (2 * CD + 2 * CB) // RING
TURNS_OUT = 2 * CD // RING
CONV_TURN = NP * TURNS_BRANCH
MERGE_TURN = 2 * CONV_TURN
OUT_TURN = MERGE_TURN + NG * TURNS_MERGE
CONV_GROUP = 4 * NP
MERGE_GROUP = 2 * CONV_GROUP
OUT_GROUP = MERGE_GROUP + 4 * NG


def build(nc, x, norm_w, w_in, lb_logits, hgrn_norm_w, conv_w, w_branch_a, w_branch_b,
          gate_bias, w_out, final_norm_w, out):
    ctx = ExitStack()
    with ctx:
        def sb(name, shape, dt=F32):
            return ctx.enter_context(nc.sbuf_tensor(name, shape, dt))

        def at(name, shape, offset, dt=F32):
            return nc.alloc_sbuf_tensor_at(name, shape, dt, offset=offset)

        def sem(name):
            return ctx.enter_context(nc.semaphore(name))

        base = (nc.sbuf_base + 31) // 32 * 32
        region_u = base
        region_y = region_u + KT * 2 * T * 4
        region_m = region_y + 2 * KB * 2 * T * 4
        region_end = region_m + KT * T * 4
        ctx.enter_context(nc.sbuf_tensor("arena", [P, (region_end - nc.sbuf_base + 3) // 4], F32))
        U = at("U", [P, KT, 2 * T], region_u, F32R)
        Y = at("Y", [P, 2 * KB, 2 * T], region_y, F32R)
        XS = at("XS", [P, 2, D], region_y)
        H = at("H", [P, 2, D], region_y)
        XR = at("XR", [P, 2, D], region_y + 2 * D * 4)
        MRG = at("MRG", [P, KT, T], region_m)
        FW = at("FW", [P, D], region_m)
        SQJ = at("SQJ", [P, D // 2], region_m)
        VEC1 = at("VEC1", [P, P], region_m + 4 * D // 2)
        VEC2 = at("VEC2", [P, P], region_m + 4 * D // 2 + 4 * P)
        W2 = 2 * T
        names = ["F", "Q", "V", "G", "SF", "SG", "PRE", "K", "SUF"]
        F, Q, V, G, SF, SG, PRE, K, SUF = [at(n, [P, W2], region_m + 4 * W2 * i)
                                           for i, n in enumerate(names)]
        scr = region_m + 4 * W2 * len(names)
        KL = at("KL", [P, 2, W2], scr)
        UP = at("UP", [P, 2, T + 2], scr)
        QR = at("QR", [P, 2, T], scr + 16 * T)
        AD = at("AD", [P, 4, P], scr + 24 * T)
        AO = at("AO", [P, 2, P], scr + 32 * T)
        O = at("O", [P, W2], scr + 36 * T)
        O2 = at("O2", [P, W2], scr + 44 * T)
        RAW = [sb(f"RAW{i}", [P, KC, GW]) for i in range(RING)]
        WS = [sb(f"WS{i}", [P, KC, 2 * GW], F32R) for i in range(RING)]
        SM = [sb(f"SM{i}", [P, 2, T]) for i in range(2)]
        GA, GB, Z = [sb(n, [P, W2]) for n in ("GA", "GB", "Z")]
        MASK = sb("MASK", [P, 7 * 64])
        IDN = sb("IDN", [P, P])
        ONES = sb("ONES", [P, P])
        VT1 = sb("VT1", [P, P])
        VT2 = sb("VT2", [P, 49])
        LB = sb("LB", [P, 16])
        OMLB = sb("OMLB", [P, 16])
        LT = sb("LT", [P, 48])
        SSQ = sb("SSQ", [P, 2, NG])
        ST = sb("ST", [P, 12])
        EPT = sb("EPT", [P, 1])
        NW, HW0 = VT1[:, 0:KT], VT2[:, 48:49]

        PS = [ctx.enter_context(nc.psum_tensor(f"PS{i}", [P, 2, 512], F32)) for i in range(2)]
        SC = [ctx.enter_context(nc.psum_tensor(f"SC{i}", [P, 512], F32)) for i in range(2)]
        OB = ctx.enter_context(nc.psum_tensor("OB", [P, 512], F32))
        SS = ctx.enter_context(nc.psum_tensor("SS", [P, 512], F32))

        XB = [PS[1][:, 0, :], PS[1][:, 1, :], SC[0][:, :], SC[1][:, :], OB[:, :], SS[:, :]]
        x_bank = lambda k: XB[k // 2 % len(XB)][:, k % 2 * T:(k % 2 + 1) * T]

        raw_loaded = [sem(f"raw_loaded{i}") for i in range(RING)]
        hi_ready = sem("hi_ready")
        lo_ready = sem("lo_ready")
        w_used = sem("w_used")
        small_out = sem("small_out")
        drained = sem("drained")
        x_loaded = [sem(f"x_loaded{i}") for i in range(4)]
        vec_loaded = sem("vec_loaded")
        consts = sem("consts")
        x_sq = sem("x_sq")
        x_var = sem("x_var")
        x_std = sem("x_std")
        x_normed = sem("x_normed")
        vec_turned = sem("vec_turned")
        vec_out = sem("vec_out")
        lb_shift = sem("lb_shift")
        lb_exp = sem("lb_exp")
        x_turned = sem("x_turned")
        u_hi = sem("u_hi")
        u_ready = sem("u_ready")
        gate_f = sem("gate_f")
        gate_g = sem("gate_g")
        level_ready = sem("level_ready")
        level_done = sem("level_done")
        level_read = sem("level_read")
        o_done = sem("o_done")
        o_out = sem("o_out")
        ss_done = sem("ss_done")
        std_ready = sem("std_ready")
        y_ready = sem("y_ready")
        merge_gate = sem("merge_gate")
        merged = sem("merged")
        m_hi = sem("m_hi")
        m_ready = sem("m_ready")
        xr_loaded = [sem(f"xr_loaded{i}") for i in range(2)]
        h_ready = sem("h_ready")
        h_sq = sem("h_sq")
        tail_var = sem("tail_var")
        tail_std = sem("tail_std")
        tail_rstd = sem("tail_rstd")
        out_dve = sem("out_dve")
        out_act = sem("out_act")
        stored = sem("stored")

        block = ctx.enter_context(nc.Block())

        @block.sync
        def _(sp):
            sp.dma_start(VEC1[0:32, :], norm_w.rearrange("a (k p) -> (a k) p", p=P)).then_inc(vec_loaded, 16)
            sp.dma_start(VEC1[32:64, :], lb_logits.rearrange("a (k p) -> (a k) p", p=P)).then_inc(vec_loaded, 16)
            sp.dma_start(VEC1[64:128, :], gate_bias.rearrange("a b (k p) -> (a b k) p", p=P)).then_inc(vec_loaded, 16)
            sp.dma_start(VEC2[0:48, :], conv_w.rearrange("a b (k p) -> (a b k) p", p=P)).then_inc(vec_loaded, 16)
            sp.dma_start(VEC2[48:49, :], hgrn_norm_w).then_inc(vec_loaded, 16)
            for n in range(4):
                half, part = n // 2, n % 2
                sp.dma_start(XS[:, half, part * 2048:(part + 1) * 2048],
                             x[0, half * P:(half + 1) * P, part * 2048:(part + 1) * 2048]).then_inc(x_loaded[n], 16)

            def load(w, rows, col, turn, s, free=True):
                src = w[rows * KC * P:(rows + 1) * KC * P, bass.ds(col, GW)]
                if free:
                    sp.wait_ge(lo_ready, RING * turn + s - (RING - 1))
                sp.dma_start(RAW[s][:, :, :], src.rearrange("(k p) c -> p k c", p=P)).then_inc(raw_loaded[s], 16)

            def column(i, col):
                return i * GW + col if col else (i + 1) * GW - GW

            def branch(i, cols, turn0, first=False):
                for n, col in enumerate(cols):
                    col = column(i, col)
                    for c in range(CD):
                        load(w_in[0], c, col, turn0 + TURNS_BRANCH * i + (n * CD + c) // RING, c % RING,
                             free=not (first and n == 0 and c < RING))

            branch(0, HGRN_GROUPS, 0, first=True)
            with sp.Fori(1, NP) as i:
                branch(i, HGRN_GROUPS, 0)
            with sp.Fori(0, NP) as i:
                branch(i, CONV_GROUPS, CONV_TURN)
            with sp.Fori(0, NG) as i:
                turn = MERGE_TURN + TURNS_MERGE * i
                for n, col in enumerate((G_A, G_B)):
                    col = column(i, col)
                    for c in range(CD):
                        load(w_in[0], c, col, turn + (n * CD + c) // RING, c % RING)
                col = column(i, 0)
                for n, w in enumerate((w_branch_a, w_branch_b)):
                    for c in range(CB):
                        load(w[0], c, col, turn + (2 * CD + n * CB + c) // RING, c % RING)
            with sp.Fori(0, NG // 2) as i:
                for n in range(2):
                    col = column(i * 2 + n, 0)
                    for c in range(CD):
                        load(w_out[0], c, col, OUT_TURN + TURNS_OUT * i + (n * CD + c) // RING, c % RING)
                    if n == 0:
                        sp.wait_ge(w_used, RING * OUT_TURN)
                        sp.wait_ge(m_ready, CD)
                    cols = bass.ds(col, GW)
                    sp.dma_start(XR[:, :, cols], x[0, :, cols].rearrange("(b p) c -> p b c", p=P)).then_inc(xr_loaded[n], 16)
                    sp.dma_start(FW[:, cols], final_norm_w[cols].partition_broadcast(P)).then_inc(xr_loaded[n], 16)
            for n in range(2):
                sp.wait_ge(out_dve, n + 1)
                sp.dma_start(out[0, n * P:(n + 1) * P, 0:D // 2], H[:, n, 0:D // 2]).then_inc(stored, 16)
            for n in range(2):
                sp.wait_ge(out_act, n + 1)
                sp.dma_start(out[0, n * P:(n + 1) * P, D // 2:D], H[:, n, D // 2:D]).then_inc(stored, 16)
            sp.wait_ge(stored, 64)

        @block.gpsimd
        def _(pool):
            pool.memset(IDN[:, :], 0.0).then_inc(consts, 1)
            pool.memset(ONES[:, :], 1.0).then_inc(consts, 1)
            pool.memset(MASK[:, :], 1.0).then_inc(consts, 1)
            pool.memset(AD[:, :, :], 0.0).then_inc(consts, 1)
            pool.memset(KL[:, :, :], 0.0).then_inc(consts, 1)
            pool.memset(EPT[:, :], EPS).then_inc(consts, 1)
            pool.wait_ge(consts, 6)
            pool.affine_select(out=IDN[:, :], in_=IDN[:, :], compare_op=ALU.not_equal, fill=1.0, base=0,
                               pattern=[[-1, P]], channel_multiplier=1).then_inc(consts, 1)
            for n, m in enumerate(LEVELS[:7]):
                v = MASK[:, n * 64:(n + 1) * 64].rearrange("p (j r) -> p j r", r=m)
                pool.affine_select(out=v, in_=v, compare_op=ALU.is_ge, fill=0.0, base=0,
                                   pattern=[[-2 * m, 64 // m], [0, m]], channel_multiplier=1).then_inc(consts, 1)
                pool.wait_ge(consts, 8 + 2 * n)
                pool.affine_select(out=v, in_=v, compare_op=ALU.is_ge, fill=0.0, base=m - 1,
                                   pattern=[[2 * m, 64 // m], [0, m]], channel_multiplier=-1).then_inc(consts, 1)

        N_CONSTS = 21

        @block.scalar
        def _(act):
            for n in range(4):
                half, part = n // 2, n % 2
                act.wait_ge(x_loaded[n], 16)
                if n:
                    act.drain()
                act.activation(SQJ[:, :], XS[:, half, part * 2048:(part + 1) * 2048], ACT.Square,
                               accum_out=ST[:, n:n + 1]).then_inc(x_sq, 1)
            act.wait_ge(x_var, 1)
            act.wait_ge(consts, N_CONSTS)
            act.activation(ST[:, 6:8], ST[:, 4:6], ACT.Sqrt, bias=EPT[:, :], scale=1.0 / D).then_inc(x_std, 1)
            act.wait_ge(lb_shift, 1)
            act.activation(LT[:, 0:32], LT[:, 0:32], ACT.Exp).then_inc(lb_exp, 1)

            def hi(turn, s, free=True):
                act.wait_ge(raw_loaded[s], turn * 16 + 16)
                if free:
                    act.wait_ge(w_used, RING * turn + s - (RING - 1))
                act.activation(WS[s][:, :, 0:GW], RAW[s][:, :, :], ACT.Copy).then_inc(hi_ready, 1)

            def small_half(group, chunks, par, free=True):
                act.wait_ge(w_used, chunks)
                if free:
                    act.wait_ge(drained, group - 1)
                act.activation(SM[par][:, :, :], PS[par][:, :, T:2 * T], ACT.Copy).then_inc(small_out, 1)

            for s in range(RING):
                hi(0, s, free=False)
            act.wait_ge(vec_out, 1)
            for k in range(KT):
                if k % 2 == 0:
                    act.wait_ge(x_turned, k // 2 + 1)
                if k % 2 == 1:
                    act.wait_ge(u_ready, k)
                act.activation(U[:, k, 0:T], x_bank(k), ACT.Copy,
                               scale=NW[:, k:k + 1]).then_inc(u_hi, 1)

            def attention(a, slot):
                if slot == 1:
                    act.wait_ge(drained, 4 * a + 4)
                    act.activation(SG[:, :], G[:, :], ACT.Sigmoid).then_inc(gate_g, 1)
                if slot == 11:
                    act.wait_ge(o_done, a + 1)
                    act.activation(O2[:, :], OB[:, :], ACT.Square).then_inc(o_out, 1)
                    act.activation(O[:, :], OB[:, :], ACT.Copy).then_inc(o_out, 1)
                if slot == 13:
                    act.wait_ge(ss_done, a + 1)
                    act.activation(GA[:, :], SS[:, :], ACT.Sqrt, bias=EPT[:, :],
                                   scale=1.0 / P).then_inc(std_ready, 1)

            def branch(i, turn0, group0, a=None, first=False):
                for slot in range(SLOTS):
                    for c in (2 * slot, 2 * slot + 1):
                        hi(turn0 + TURNS_BRANCH * i + c // RING + 1, c % RING)
                    if a is not None:
                        attention(a, slot)
                    if slot == 5:
                        act.wait_ge(drained, group0 + 4 * i + 1)
                        act.activation(SF[:, :], F[:, :], ACT.Sigmoid).then_inc(gate_f, 1)
                    if slot % 4 == 3:
                        n = slot // 4
                        small_half(group0 + 4 * i + n, RING * (turn0 + TURNS_BRANCH * i) + CD * (n + 1), n % 2, free=not (first and n < 2))

            branch(0, 0, 0, first=True)
            with act.Fori(1, NP) as i:
                branch(i, 0, 0, a=i - 1)
            branch(0, CONV_TURN, CONV_GROUP, a=NP - 1)
            with act.Fori(1, NP) as i:
                branch(i, CONV_TURN, CONV_GROUP)

            def merge(i, last=False):
                turn = MERGE_TURN + TURNS_MERGE * i + 1
                group = MERGE_GROUP + 4 * i
                chunks = RING * (MERGE_TURN + TURNS_MERGE * i)
                for c in range(2 * CD + 2 * CB):
                    hi(turn + c // RING, c % RING)
                    if c in (CD + 2, 2 * CD + 2):
                        n = c // CD - 1
                        act.wait_ge(drained, group + n + 1)
                        for t in range(2):
                            gate = (GA, GB)[n][:, t * T:(t + 1) * T]
                            act.activation(gate, gate, ACT.Sigmoid,
                                           bias=VT1[:, bass.ds(i * 2 + (64 + n * KT + t), 1)]).then_inc(merge_gate, 1)
                    if c == CD - 1:
                        small_half(group, chunks + c + 1, 0)
                    if c == 2 * CD - 1:
                        small_half(group + 1, chunks + c + 1, 1)
                    if last and c > 2 * CD:
                        split_merged(c - 2 * CD - 1)
                    if c == 2 * CD + CB - 1:
                        small_half(group + 2, chunks + c + 1, 0)
                    if c == 2 * CD + 2 * CB - 1:
                        small_half(group + 3, chunks + c + 1, 1)

            def split_merged(n):
                act.wait_ge(w_used, RING * OUT_TURN - 2 * CB)
                act.wait_ge(merged, 2 * n + 2)
                act.activation(U[:, KC * n:KC * (n + 1), 0:T], MRG[:, KC * n:KC * (n + 1), :], ACT.Copy).then_inc(m_hi, 1)

            with act.Fori(0, NG - 1) as i:
                merge(i)
            merge(NG - 1, last=True)
            split_merged(CD - 1)

            def output(i, last=False):
                for n in range(2):
                    for c in range(CD if not (last and n == 1) else RING):
                        hi(OUT_TURN + TURNS_OUT * i + (n * CD + c) // RING + 1, c % RING)
                    small_half(OUT_GROUP + 2 * i + n, RING * (OUT_TURN + TURNS_OUT * i) + CD * (n + 1), n)
                    act.wait_ge(h_ready, 2 * i + n + 1)
                    for b in range(2):
                        act.activation(SM[n][:, b, :], (GA, GB)[n][:, b * T:(b + 1) * T], ACT.Square,
                                       accum_out=SSQ[:, b, bass.ds(i * 2 + n, 1)]).then_inc(h_sq, 1)

            with act.Fori(0, NG // 2 - 1) as i:
                output(i)
            output(NG // 2 - 1, last=True)
            act.wait_ge(tail_var, 1)
            act.activation(ST[:, 6:8], ST[:, 4:6], ACT.Sqrt, bias=EPT[:, :], scale=1.0 / D).then_inc(tail_std, 1)
            act.wait_ge(tail_rstd, 1)
            for b in range(2):
                act.activation(H[:, b, D // 2:D], H[:, b, D // 2:D], ACT.Copy, scale=ST[:, 8 + b:9 + b]).then_inc(out_act, 1)

        @block.vector
        def _(dve):
            def after():
                dve.drain()

            def rstd_small(r, std, var, tmp, n):
                dve.reciprocal(r, std)
                after()
                dve.tensor_tensor(tmp, r, r, ALU.mult)
                after()
                dve.tensor_tensor(tmp, tmp, var, ALU.mult)
                after()
                dve.tensor_scalar(tmp, tmp, -0.5, 1.5, ALU.mult, ALU.add)
                after()
                dve.tensor_tensor(r, r, tmp, ALU.mult)
                after()

            dve.wait_ge(x_sq, 4)
            dve.tensor_tensor(ST[:, 4:6], ST[:, 0:4:2], ST[:, 1:4:2], ALU.add).then_inc(x_var, 1)
            dve.wait_ge(vec_turned, 1)
            dve.tensor_copy(VT1[:, :], SC[0][:, 0:P])
            dve.tensor_copy(VT2[:, :], SC[0][:, P:P + 49]).then_inc(vec_out, 1)
            after()
            dve.tensor_tensor(LT[:, 32:48], VT1[:, 32:48], VT1[:, 48:64], ALU.max)
            after()
            dve.tensor_tensor(LT[:, 0:16], VT1[:, 32:48], LT[:, 32:48], ALU.subtract)
            dve.tensor_tensor(LT[:, 16:32], VT1[:, 48:64], LT[:, 32:48], ALU.subtract).then_inc(lb_shift, 1)
            dve.wait_ge(x_std, 1)
            dve.tensor_scalar(ST[:, 4:6], ST[:, 4:6], 1.0 / D, EPS, ALU.mult, ALU.add)
            after()
            rstd_small(ST[:, 8:10], ST[:, 6:8], ST[:, 4:6], ST[:, 10:12], 2)
            for b in range(2):
                dve.tensor_scalar(XS[:, b, :], XS[:, b, :], ST[:, 8 + b:9 + b], None, ALU.mult).then_inc(x_normed, 1)

            dve.wait_ge(consts, N_CONSTS)

            def lo(turn, s):
                dve.wait_ge(hi_ready, RING * turn + s + 1)
                dve.tensor_tensor(WS[s][:, :, GW:2 * GW], RAW[s][:, :, :], WS[s][:, :, 0:GW],
                                  ALU.subtract).then_inc(lo_ready, 1)

            for s in range(RING):
                lo(0, s)
            dve.wait_ge(lb_exp, 1)
            dve.tensor_tensor(LT[:, 32:48], LT[:, 0:16], LT[:, 16:32], ALU.add)
            after()
            dve.reciprocal(LT[:, 32:48], LT[:, 32:48])
            after()
            dve.tensor_tensor(LB[:, :], LT[:, 0:16], LT[:, 32:48], ALU.mult)
            after()
            dve.tensor_scalar(OMLB[:, :], LB[:, :], -1.0, 1.0, ALU.mult, ALU.add)
            for k in range(KT):
                dve.wait_ge(u_hi, k + 1)
                dve.scalar_tensor_tensor(U[:, k, T:2 * T], x_bank(k), NW[:, k:k + 1],
                                         U[:, k, 0:T], ALU.mult, ALU.subtract).then_inc(u_ready, 1)

            def drain_group(dst, group, par):
                dve.wait_ge(small_out, group + 1)
                dve.tensor_tensor(dst, PS[par][:, :, 0:T], SM[par][:, :, :], ALU.add).then_inc(drained, 1)

            def pair(t):
                return t[:, :].rearrange("p (t n) -> p t n", t=2)

            def store_y(y, kt):
                ys = Y[:, bass.ds(kt, 2), :]
                dve.tensor_copy(ys[:, :, 0:T], y)
                after()
                dve.tensor_tensor(ys[:, :, T:2 * T], y, ys[:, :, 0:T], ALU.subtract).then_inc(y_ready, 1)

            def halves(t, m):
                v = t.rearrange("p (n two m) -> p n two m", two=2, m=m)
                return v[:, :, 0, :], v[:, :, 1, :]

            def produce(n):
                m = LEVELS[n]
                blocks = W2 // (2 * m)
                qr = QR[:, n % 2, :].rearrange("p (n m) -> p n m", m=m)
                q_right = halves(Q[:, :], m)[1]
                p_left, p_right = halves(PRE[:, :], m)
                s_left, s_right = halves(SUF[:, :], m)
                op = dve.tensor_tensor(qr, q_right, p_right, ALU.mult)
                if m > 1:
                    op = dve.tensor_tensor(halves(KL[:, n % 2, :], m)[0], halves(K[:, :], m)[0], s_left, ALU.mult)
                op.then_inc(level_ready, 1)
                if m == T // 2:
                    return
                over_right = p_right[:, :, m - 1:m].broadcast_to([P, blocks, m])
                over_left = p_left[:, :, m - 1:m].broadcast_to([P, blocks, m])
                if m == 1:
                    dve.memset(s_right, 1.0)
                    dve.tensor_copy(s_left, over_right)
                else:
                    dve.tensor_tensor(s_left, s_left, over_right, ALU.mult)
                after()
                dve.tensor_tensor(p_right, p_right, over_left, ALU.mult)
                after()

            def consume(a, n):
                m = LEVELS[n]
                if m == P:
                    dve.tensor_copy(AO[:, :, :], SC[n % 2][:, 0:T].rearrange("p (h t) -> p h t", h=2)).then_inc(level_read, 1)
                    return
                if n == 0:
                    eye = IDN[:, :].bitcast(U32).unsqueeze(1).broadcast_to([P, 4, P])
                    dve.copy_predicated(AD[:, :, :], eye, SS[:, :].rearrange("p (g t) -> p g t", g=4))
                after()
                dst = AD[:, :, :].rearrange("p g (j two r) -> p g j two r", two=2, r=m)[:, :, :, 1, :]
                data = SC[n % 2][:, 0:T].rearrange("p (g j r) -> p g j r", g=4, r=m)
                mask = MASK[:, n * 64:(n + 1) * 64].bitcast(U32).rearrange("p (j r) -> p j r", r=m)
                mask = mask.unsqueeze(1).broadcast_to([P, 4, 64 // m, m])
                dve.copy_predicated(dst, mask, data).then_inc(level_read, 1)

            def attention(a, slot):
                if slot == 0:
                    dve.wait_ge(gate_f, a + 1)
                    for h in range(2):
                        one = bass.ds(a * 2 + h, 1)
                        dve.tensor_scalar(PRE[:, h * T:(h + 1) * T], SF[:, h * T:(h + 1) * T], OMLB[:, one],
                                          LB[:, one], ALU.mult, ALU.add)
                    after()
                    dve.tensor_scalar(K[:, :], PRE[:, :], -1.0, 1.0, ALU.mult, ALU.add)
                if 2 <= slot < 10:
                    consume(a, slot - 2)
                if slot < 8:
                    produce(slot)
                if slot == 14:
                    dve.wait_ge(std_ready, a + 1)
                    dve.tensor_scalar(Z[:, :], SS[:, :], 1.0 / P, EPS, ALU.mult, ALU.add)
                    dve.reciprocal(GB[:, :], GA[:, :])
                    after()
                    dve.tensor_tensor(Z[:, :], Z[:, :], GB[:, :], ALU.mult)
                    after()
                    dve.tensor_tensor(Z[:, :], Z[:, :], GB[:, :], ALU.mult)
                    after()
                    dve.tensor_scalar(Z[:, :], Z[:, :], -0.5, 1.5, ALU.mult, ALU.add)
                    after()
                    dve.tensor_tensor(GB[:, :], GB[:, :], Z[:, :], ALU.mult)
                    after()
                if slot == 15:
                    dve.wait_ge(o_out, 2 * a + 2)
                    dve.wait_ge(gate_g, a + 1)
                    dve.scalar_tensor_tensor(O[:, :], O[:, :], HW0, GB[:, :], ALU.mult, ALU.mult)
                    dve.tensor_tensor(SG[:, :], SG[:, :], G[:, :], ALU.mult)
                    after()
                    dve.tensor_tensor(O[:, :], O[:, :], SG[:, :], ALU.mult)
                    after()
                    store_y(pair(O), a * 2)

            def conv(i, slot):
                if slot == 8:
                    dve.wait_ge(gate_f, NP + i + 1)
                    dve.tensor_tensor(SF[:, :], SF[:, :], F[:, :], ALU.mult)
                if slot == 12:
                    dve.memset(UP[:, :, 0:2], 0.0)
                    dve.tensor_tensor(UP[:, :, 2:T + 2], pair(Q), pair(V), ALU.mult)
                    after()
                if slot == 13:
                    for j in range(3):
                        for t in range(2):
                            tap = VT2[:, bass.ds(i * 2 + (16 * j + t), 1)]
                            acc = K[:, t * T:(t + 1) * T]
                            if j == 0:
                                dve.tensor_scalar(acc, UP[:, t, j:T + j], tap, None, ALU.mult)
                            else:
                                dve.scalar_tensor_tensor(acc, UP[:, t, j:T + j], tap, acc, ALU.mult, ALU.add)
                        after()

            def branch(i, turn0, group0, a=None, is_conv=False):
                for slot in range(SLOTS):
                    for c in (2 * slot, 2 * slot + 1):
                        if a is not None and c == 2 * slot + 1 and 2 <= slot < 10:
                            dve.wait_ge(level_done, 8 * a + slot - 1)
                        lo(turn0 + TURNS_BRANCH * i + c // RING + 1, c % RING)
                    if a is not None:
                        attention(a, slot)
                    if is_conv:
                        conv(i, slot)
                    if slot % 4 == 3:
                        n = slot // 4
                        after()
                        if n == 2 and a is not None:
                            dve.wait_ge(o_done, a + 1)
                        drain_group(pair((F, Q, V, G)[n]), group0 + 4 * i + n, n % 2)
                        after()
                if is_conv:
                    dve.tensor_tensor(K[:, :], K[:, :], G[:, :], ALU.mult)
                    after()
                    dve.tensor_tensor(K[:, :], K[:, :], SF[:, :], ALU.mult)
                    after()
                    store_y(pair(K), i * 2 + KB)
                    after()

            branch(0, 0, 0)
            with dve.Fori(1, NP) as i:
                branch(i, 0, 0, a=i - 1)
            branch(0, CONV_TURN, CONV_GROUP, a=NP - 1, is_conv=True)
            with dve.Fori(1, NP) as i:
                branch(i, CONV_TURN, CONV_GROUP, is_conv=True)

            def split_merged(n):
                dve.wait_ge(m_hi, n + 1)
                k = slice(KC * n, KC * (n + 1))
                dve.tensor_tensor(U[:, k, T:2 * T], MRG[:, k, :], U[:, k, 0:T], ALU.subtract).then_inc(m_ready, 1)

            def merge(i, last=False):
                turn = MERGE_TURN + TURNS_MERGE * i + 1
                group = MERGE_GROUP + 4 * i
                out2 = MRG[:, bass.ds(i * 2, 2), :]
                for c in range(2 * CD + 2 * CB):
                    lo(turn + c // RING, c % RING)
                    if c == CD - 1:
                        drain_group(pair(GA), group, 0)
                    if c == 2 * CD - 1:
                        drain_group(pair(GB), group + 1, 1)
                    if last and c > 2 * CD:
                        split_merged(c - 2 * CD - 1)
                    if c == 2 * CD + CB - 1:
                        drain_group(pair(Z), group + 2, 0)
                        after()
                        dve.wait_ge(merge_gate, 4 * i + 2)
                        dve.tensor_tensor(out2, pair(GA), pair(Z), ALU.mult)
                        after()
                drain_group(pair(Z), group + 3, 1)
                after()
                dve.wait_ge(merge_gate, 4 * i + 4)
                dve.tensor_tensor(Z[:, :], GB[:, :], Z[:, :], ALU.mult)
                after()
                dve.tensor_tensor(out2, out2, pair(Z), ALU.add).then_inc(merged, 1)
                after()

            with dve.Fori(0, NG - 1) as i:
                merge(i)
            merge(NG - 1, last=True)
            split_merged(CD - 1)

            def output(i, first=False, last=False):
                for n in range(2):
                    for c in range(CD if not (last and n == 1) else RING):
                        lo(OUT_TURN + TURNS_OUT * i + (n * CD + c) // RING + 1, c % RING)
                    h = pair((GA, GB)[n])
                    if not first:
                        dve.wait_ge(h_sq, 4 * i + 2 * n - 2)
                    drain_group(h, OUT_GROUP + 2 * i + n, n)
                    after()
                    cols = bass.ds(i * 2 * GW + n * GW, GW)
                    dve.wait_ge(xr_loaded[n], i * 32 + 32)
                    dve.tensor_tensor(h, h, XR[:, :, cols], ALU.add).then_inc(h_ready, 1)
                    after()
                    fw = FW[:, cols].unsqueeze(1).broadcast_to([P, 2, GW])
                    dve.tensor_tensor(H[:, :, cols], h, fw, ALU.mult)

            output(0, first=True)
            with dve.Fori(1, NG // 2 - 1) as i:
                output(i)
            output(NG // 2 - 1, last=True)
            dve.wait_ge(h_sq, 2 * NG)
            dve.tensor_reduce(ST[:, 4:6], SSQ[:, :, :], AX.X, ALU.add).then_inc(tail_var, 1)
            dve.wait_ge(tail_std, 1)
            dve.tensor_scalar(ST[:, 4:6], ST[:, 4:6], 1.0 / D, EPS, ALU.mult, ALU.add)
            after()
            rstd_small(ST[:, 8:10], ST[:, 6:8], ST[:, 4:6], ST[:, 10:12], 2)
            dve.tensor_copy(ST[:, 0:2], ST[:, 8:10]).then_inc(tail_rstd, 1)
            for b in range(2):
                dve.tensor_scalar(H[:, b, 0:D // 2], H[:, b, 0:D // 2], ST[:, 8 + b:9 + b], None,
                                  ALU.mult).then_inc(out_dve, 1)

        @block.tensor
        def _(pe):
            pe.wait_ge(consts, N_CONSTS)
            pe.wait_ge(vec_loaded, 80)
            pe.transpose(SC[0][:, 0:P], VEC1[:, :], IDN[:, :])
            pe.transpose(SC[0][:, P:P + 49], VEC2[0:49, :], IDN[0:49, 0:49]).then_inc(vec_turned, 1)
            pe.wait_ge(x_normed, 2)
            pe.wait_ge(vec_out, 1)

            def turn_x(k2):
                if k2 >= len(XB):
                    pe.wait_ge(u_ready, 2 * (k2 - len(XB)) + 2)
                for k in (2 * k2, 2 * k2 + 1):
                    for b in range(2):
                        op = pe.transpose(x_bank(k)[:, b * P:(b + 1) * P], XS[:, b, k * P:(k + 1) * P], IDN[:, :])
                op.then_inc(x_turned, 1)

            for k2 in range(len(XB)):
                turn_x(k2)

            def split_product(bank, stat_hi, stat_lo, both, first, last):
                def with_lo(stop):
                    return pe.matmul(bank[:, T:2 * T], stat_lo, both[:, 0:T], start=False, stop=stop,
                                     skip_group_check=True)

                if not first:
                    with_lo(False)
                op = pe.matmul(bank, stat_hi, both, start=first, stop=last, skip_group_check=True)
                return with_lo(False) if first else op

            def channels(par, s, rhs, k0, n_tiles):
                for k in range(KC):
                    for t in range(2):
                        op = split_product(PS[par][:, t, :], WS[s][:, k, t * P:(t + 1) * P],
                                           WS[s][:, k, GW + t * P:GW + (t + 1) * P], rhs[:, k0 + k, :],
                                           k0 + k == 0, k0 + k == n_tiles - 1)
                return op

            def positions(par, s, lhs, k0, n_tiles):
                for k in range(KC):
                    for b in range(2):
                        op = split_product(PS[par][:, b, :], lhs[:, k0 + k, b * P:(b + 1) * P],
                                           lhs[:, k0 + k, T + b * P:T + (b + 1) * P], WS[s][:, k, :],
                                           k0 + k == 0, k0 + k == n_tiles - 1)
                return op

            def attention(a, c):
                if c % 2 == 0 and 4 <= c < 20:
                    n = (c - 4) // 2
                    pe.wait_ge(level_ready, 8 * a + (n + 1))
                    if n >= 2:
                        pe.wait_ge(level_read, 8 * a + (n - 1))
                    if n == 7:
                        for h in range(2):
                            op = pe.matmul(SC[n % 2][:, h * P:(h + 1) * P], KL[:, n % 2, h * T:h * T + P],
                                           QR[:, n % 2, h * P:(h + 1) * P], start=True, stop=True)
                    else:
                        for g in range(4):
                            k_side = (K[:, :] if n == 0 else KL[:, n % 2, :])[:, g * P:(g + 1) * P]
                            op = pe.matmul(SC[n % 2][:, g * 64:(g + 1) * 64], k_side,
                                           QR[:, n % 2, g * 64:(g + 1) * 64], start=True, stop=True)
                            if n == 0:
                                op = pe.matmul(SS[:, g * P:(g + 1) * P], k_side, Q[:, g * P:(g + 1) * P],
                                               start=True, stop=True)
                    op.then_inc(level_done, 1)
                if c == 22:
                    pe.wait_ge(level_read, 8 * a + 8)
                    for h in range(2):
                        v = [V[:, b * T + h * P:b * T + (h + 1) * P] for b in range(2)]
                        pe.matmul(OB[:, h * T:h * T + P], v[0], AD[:, 2 * h, :], start=True, stop=True)
                        pe.matmul(OB[:, h * T + P:(h + 1) * T], v[0], AO[:, h, :], start=True, stop=False)
                        op = pe.matmul(OB[:, h * T + P:(h + 1) * T], v[1], AD[:, 2 * h + 1, :], start=False, stop=True)
                    op.then_inc(o_done, 1)
                if c == 26:
                    pe.wait_ge(o_out, 2 * a + 1)
                    pe.matmul(SS[:, :], ONES[:, :], O2[:, :], start=True, stop=True).then_inc(ss_done, 1)

            def group(turn, n0, n_chunks, mode, operand, k_start, par, gidx, free=True, u_wait=None, a=None):
                if free:
                    pe.wait_ge(drained, gidx - 1)
                for c in range(n_chunks):
                    if u_wait is not None and u_wait[0] is u_ready:
                        left = KT // 2 - len(XB)
                        for k2 in range(left * (c - 1) // (RING - 1), left * c // (RING - 1)):
                            if 0 <= k2 < left:
                                turn_x(len(XB) + k2)
                    if u_wait is not None:
                        pe.wait_ge(u_wait[0], u_wait[1] * (c + 1))
                    at_chunk = n0 + c
                    pe.wait_ge(lo_ready, RING * (turn + at_chunk // RING) + at_chunk % RING + 1)
                    op = mode(par, at_chunk % RING, operand[:, k_start:k_start + n_chunks * KC, :], c * KC,
                              n_chunks * KC)
                    op.then_inc(w_used, 1)
                    if a is not None:
                        attention(a, at_chunk)

            def branch(i, turn0, group0, modes, a=None, first=False):
                for n in range(4):
                    group(turn0 + TURNS_BRANCH * i, n * CD, CD, modes[n], U, 0, n % 2, group0 + 4 * i + n,
                          free=not (first and n < 2), u_wait=(u_ready, KC) if first and n == 0 else None, a=a)

            hgrn = (channels, channels, positions, channels)
            branch(0, 0, 0, hgrn, first=True)
            with pe.Fori(1, NP) as i:
                branch(i, 0, 0, hgrn, a=i - 1)
            branch(0, CONV_TURN, CONV_GROUP, (channels,) * 4, a=NP - 1)
            with pe.Fori(1, NP) as i:
                branch(i, CONV_TURN, CONV_GROUP, (channels,) * 4)
            pe.wait_ge(y_ready, 2 * NP)
            with pe.Fori(0, NG) as i:
                turn, g = MERGE_TURN + TURNS_MERGE * i, MERGE_GROUP + 4 * i
                group(turn, 0, CD, channels, U, 0, 0, g)
                group(turn, CD, CD, channels, U, 0, 1, g + 1)
                group(turn, 2 * CD, CB, channels, Y, 0, 0, g + 2)
                group(turn, 2 * CD + CB, CB, channels, Y, KB, 1, g + 3)

            def output(i, first=False):
                for n in range(2):
                    group(OUT_TURN + TURNS_OUT * i, n * CD, CD, positions, U, 0, n, OUT_GROUP + 2 * i + n,
                          u_wait=(m_ready, 1) if first and n == 0 else None)

            output(0, first=True)
            with pe.Fori(1, NG // 2) as i:
                output(i)


_INS = ["x", "norm_w", "w_in", "lb_logits", "hgrn_norm_w", "conv_w", "w_branch_a", "w_branch_b",
        "gate_bias", "w_out", "final_norm_w"]


def kernel(**inputs):
    import numpy as np
    import concourse.bacc as bacc
    from concourse import mybir as mb
    from concourse.bass_utils import run_bass_kernel_spmd

    nc = bacc.Bacc("TRN2", target_bir_lowering=False, num_devices=1, dynamic_dma_scratch_size=1024)
    arrays, args = {}, []
    for name in _INS:
        a = np.ascontiguousarray(inputs[name])
        arrays[f"in_{name}"] = a
        args.append(nc.dram_tensor(f"in_{name}", a.shape, mb.dt.from_np(a.dtype), kind="ExternalInput").ap())
    out = nc.dram_tensor("out_dram", (1, T, D), F32, kind="ExternalOutput").ap()
    build(nc, *args, out)
    r = run_bass_kernel_spmd(nc, [arrays], core_ids=[0])
    return r.results[0]["out_dram"]
```

```python
import concourse.bass as bass
from concourse import mybir
from contextlib import ExitStack

F32 = mybir.dt.float32
F32R = mybir.dt.float32r
U32 = mybir.dt.uint32
ALU = mybir.AluOpType
ACT = mybir.ActivationFunctionType
AX = mybir.AxisListType

P = 128
T = 256
D = 4096
KT = D // P
BW = 2048
KB = BW // P
GW = 256
KC = 4
RING = 4
CD, CB = KT // KC, KB // KC
NP = BW // GW
NG = D // GW
XC = 1024
EARLY = 3
SLOTS = 16
LEVELS = (1, 2, 4, 8, 16, 32, 64, 128)
EPS = 1e-6
A_Q, A_F, A_I, A_G, C_B, C_C, C_H, C_G = (BW * n for n in range(8))
G_A, G_B = 8 * BW, 8 * BW + D
HGRN_GROUPS = (A_F, A_Q, A_I, A_G)
CONV_GROUPS = (C_G, C_C, C_H, C_B)
TURNS_BRANCH = 4 * CD // RING
TURNS_MERGE = (2 * CD + 2 * CB) // RING
TURNS_OUT = 2 * CD // RING
CONV_TURN = NP * TURNS_BRANCH
MERGE_TURN = 2 * CONV_TURN
OUT_TURN = MERGE_TURN + NG * TURNS_MERGE
CONV_GROUP = 4 * NP
MERGE_GROUP = 2 * CONV_GROUP
OUT_GROUP = MERGE_GROUP + 4 * NG


def build(nc, x, norm_w, w_in, lb_logits, hgrn_norm_w, conv_w, w_branch_a, w_branch_b,
          gate_bias, w_out, final_norm_w, out):
    ctx = ExitStack()
    with ctx:
        def sb(name, shape, dt=F32):
            return ctx.enter_context(nc.sbuf_tensor(name, shape, dt))

        def at(name, shape, offset, dt=F32):
            return nc.alloc_sbuf_tensor_at(name, shape, dt, offset=offset)

        def sem(name):
            return ctx.enter_context(nc.semaphore(name))

        base = (nc.sbuf_base + 31) // 32 * 32
        region_u = base
        region_y = region_u + KT * 2 * T * 4
        region_m = region_y + 2 * KB * 2 * T * 4
        region_end = region_m + KT * T * 4
        ctx.enter_context(nc.sbuf_tensor("arena", [P, (region_end - nc.sbuf_base + 3) // 4], F32))
        U = at("U", [P, KT, 2 * T], region_u, F32R)
        Y = at("Y", [P, 2 * KB, 2 * T], region_y, F32R)
        XS = at("XS", [P, 2, D], region_y)
        H = at("H", [P, 2, D], region_y)
        XR = at("XR", [P, 2, D], region_y + 2 * D * 4)
        MRG = at("MRG", [P, KT, T], region_m)
        FW = at("FW", [P, D], region_m)
        SQA = at("SQA", [P, XC], region_m)
        SQD = at("SQD", [P, XC], region_m + 4 * XC)
        VEC1 = at("VEC1", [P, P], region_m + 8 * XC)
        VEC2 = at("VEC2", [P, P], region_m + 8 * XC + 4 * P)
        W2 = 2 * T
        names = ["F", "Q", "V", "G", "SF", "SG", "PRE", "K", "SUF"]
        F, Q, V, G, SF, SG, PRE, K, SUF = [at(n, [P, W2], region_m + 4 * W2 * i)
                                           for i, n in enumerate(names)]
        scr = region_m + 4 * W2 * len(names)
        KL = at("KL", [P, 2, W2], scr)
        UP = at("UP", [P, 2, T + 2], scr)
        QR = at("QR", [P, 2, T], scr + 16 * T)
        AD = at("AD", [P, 4, P], scr + 24 * T)
        AO = at("AO", [P, 2, P], scr + 32 * T)
        O = at("O", [P, W2], scr + 36 * T)
        O2 = at("O2", [P, W2], scr + 44 * T)
        RAW = [sb(f"RAW{i}", [P, KC, GW]) for i in range(RING)]
        WS = [sb(f"WS{i}", [P, KC, 2 * GW], F32R) for i in range(RING)]
        SM = [sb(f"SM{i}", [P, 2, T]) for i in range(2)]
        GA, GB, Z = [sb(n, [P, W2]) for n in ("GA", "GB", "Z")]
        MASK = sb("MASK", [P, 7 * 64])
        IDN = sb("IDN", [P, P])
        ONES = sb("ONES", [P, P])
        VT1 = sb("VT1", [P, P])
        VT2 = sb("VT2", [P, 49])
        LB = sb("LB", [P, 16])
        OMLB = sb("OMLB", [P, 16])
        LT = sb("LT", [P, 48])
        SSQ = sb("SSQ", [P, 2, NG])
        ST = sb("ST", [P, 20])
        RS = sb("RS", [P, 4, 4])
        EPT = sb("EPT", [P, 1])
        NW, HW0 = VT1[:, 0:KT], VT2[:, 48:49]

        PS = [ctx.enter_context(nc.psum_tensor(f"PS{i}", [P, 2, 512], F32)) for i in range(2)]
        SC = [ctx.enter_context(nc.psum_tensor(f"SC{i}", [P, 512], F32)) for i in range(2)]
        OB = ctx.enter_context(nc.psum_tensor("OB", [P, 512], F32))
        SS = ctx.enter_context(nc.psum_tensor("SS", [P, 512], F32))

        XB = [b[:, 0:T] for b in (PS[1][:, 0, :], PS[1][:, 1, :], SC[0], SC[1], OB, SS)]

        EPS_WRITTEN, IDN_WRITTEN, N_CONSTS = 1, 3, 21

        raw_loaded = [sem(f"raw_loaded{i}") for i in range(RING)]
        hi_ready = sem("hi_ready")
        lo_ready = sem("lo_ready")
        w_used = sem("w_used")
        small_out = sem("small_out")
        drained = sem("drained")
        x_loaded = [sem(f"x_loaded{i}") for i in range(2 * D // XC)]
        vec_loaded = sem("vec_loaded")
        consts = sem("consts")
        x_sq = sem("x_sq")
        x_var = sem("x_var")
        x_std = sem("x_std")
        x_rstd = sem("x_rstd")
        x_norm_dve = sem("x_norm_dve")
        x_norm_act = sem("x_norm_act")
        vec_turned = sem("vec_turned")
        vec_out = sem("vec_out")
        lb_shift = sem("lb_shift")
        lb_exp = sem("lb_exp")
        lb_ready = sem("lb_ready")
        x_turned = sem("x_turned")
        u_hi = sem("u_hi")
        u_ready = sem("u_ready")
        gate_f = sem("gate_f")
        gate_g = sem("gate_g")
        level_ready = sem("level_ready")
        level_done = sem("level_done")
        level_read = sem("level_read")
        o_done = sem("o_done")
        o_out = sem("o_out")
        ss_done = sem("ss_done")
        std_ready = sem("std_ready")
        rstd_ready = sem("rstd_ready")
        rstd_spread = sem("rstd_spread")
        y_ready = sem("y_ready")
        merge_gate = sem("merge_gate")
        merged = sem("merged")
        m_hi = sem("m_hi")
        m_ready = sem("m_ready")
        xr_loaded = [sem(f"xr_loaded{i}") for i in range(2)]
        h_ready = sem("h_ready")
        h_sq = sem("h_sq")
        tail_var = sem("tail_var")
        tail_std = sem("tail_std")
        tail_rstd = sem("tail_rstd")
        out_dve = sem("out_dve")
        out_act = sem("out_act")
        stored = sem("stored")

        OUT_PIECES = [(0, 0, out_dve, 1), (1, 0, out_dve, 2), (0, 1, out_act, 1), (1, 1, out_dve, 3),
                      (0, 2, out_dve, 4), (1, 2, out_act, 2), (0, 3, out_dve, 5), (1, 3, out_act, 3)]

        block = ctx.enter_context(nc.Block())

        @block.sync
        def _(sp):
            for n in range(2 * D // XC):
                half, cols = n % 2, slice(n // 2 * XC, (n // 2 + 1) * XC)
                sp.dma_start(XS[:, half, cols], x[0, half * P:(half + 1) * P, cols]).then_inc(x_loaded[n], 16)

            def load(w, rows, col, turn, s, free=True):
                src = w[rows * KC * P:(rows + 1) * KC * P, bass.ds(col, GW)]
                if free:
                    sp.wait_ge(lo_ready, RING * turn + s - (RING - 1))
                sp.dma_start(RAW[s][:, :, :], src.rearrange("(k p) c -> p k c", p=P)).then_inc(raw_loaded[s], 16)

            def column(i, col):
                return i * GW + col if col else (i + 1) * GW - GW

            def branch(i, cols, turn0, first=False):
                for n, col in enumerate(cols):
                    col = column(i, col)
                    for c in range(CD):
                        load(w_in[0], c, col, turn0 + TURNS_BRANCH * i + (n * CD + c) // RING, c % RING,
                             free=not (first and n == 0 and c < RING))

            branch(0, HGRN_GROUPS, 0, first=True)
            with sp.Fori(1, NP) as i:
                branch(i, HGRN_GROUPS, 0)
            with sp.Fori(0, NP) as i:
                branch(i, CONV_GROUPS, CONV_TURN)
            with sp.Fori(0, NG) as i:
                turn = MERGE_TURN + TURNS_MERGE * i
                for n, col in enumerate((G_A, G_B)):
                    col = column(i, col)
                    for c in range(CD):
                        load(w_in[0], c, col, turn + (n * CD + c) // RING, c % RING)
                col = column(i, 0)
                for n, w in enumerate((w_branch_a, w_branch_b)):
                    for c in range(CB):
                        load(w[0], c, col, turn + (2 * CD + n * CB + c) // RING, c % RING)
            with sp.Fori(0, NG // 2) as i:
                for n in range(2):
                    col = column(i * 2 + n, 0)
                    for c in range(CD):
                        load(w_out[0], c, col, OUT_TURN + TURNS_OUT * i + (n * CD + c) // RING, c % RING)
                    if n == 0:
                        sp.wait_ge(w_used, RING * OUT_TURN)
                        sp.wait_ge(m_ready, CD)
                    cols = bass.ds(col, GW)
                    sp.dma_start(XR[:, :, cols], x[0, :, cols].rearrange("(b p) c -> p b c", p=P)).then_inc(xr_loaded[n], 16)
                    sp.dma_start(FW[:, cols], final_norm_w[cols].partition_broadcast(P)).then_inc(xr_loaded[n], 16)
            for half, c, done, count in OUT_PIECES:
                sp.wait_ge(done, count)
                cols = slice(c * XC, (c + 1) * XC)
                sp.dma_start(out[0, half * P:(half + 1) * P, cols], H[:, half, cols]).then_inc(stored, 16)
            sp.wait_ge(stored, 16 * len(OUT_PIECES))

        @block.gpsimd
        def _(pool):
            pool.memset(EPT[:, :], EPS).then_inc(consts, 1)
            pool.memset(IDN[:, :], 0.0).then_inc(consts, 1)
            pool.wait_ge(consts, 2)
            pool.affine_select(out=IDN[:, :], in_=IDN[:, :], compare_op=ALU.not_equal, fill=1.0, base=0,
                               pattern=[[-1, P]], channel_multiplier=1).then_inc(consts, 1)
            pool.memset(MASK[:, :], 1.0).then_inc(consts, 1)
            pool.memset(ONES[:, :], 1.0).then_inc(consts, 1)
            pool.memset(AD[:, :, :], 0.0).then_inc(consts, 1)
            pool.memset(KL[:, :, :], 0.0).then_inc(consts, 1)
            pool.wait_ge(consts, 7)
            for n, m in enumerate(LEVELS[:7]):
                v = MASK[:, n * 64:(n + 1) * 64].rearrange("p (j r) -> p j r", r=m)
                pool.affine_select(out=v, in_=v, compare_op=ALU.is_ge, fill=0.0, base=0,
                                   pattern=[[-2 * m, 64 // m], [0, m]], channel_multiplier=1).then_inc(consts, 1)
                pool.wait_ge(consts, 8 + 2 * n)
                pool.affine_select(out=v, in_=v, compare_op=ALU.is_ge, fill=0.0, base=m - 1,
                                   pattern=[[2 * m, 64 // m], [0, m]], channel_multiplier=-1).then_inc(consts, 1)


        @block.scalar
        def _(act):
            act.dma_start(VEC1[0:32, :], norm_w.rearrange("a (k p) -> (a k) p", p=P)).then_inc(vec_loaded, 16)
            act.dma_start(VEC1[32:64, :], lb_logits.rearrange("a (k p) -> (a k) p", p=P)).then_inc(vec_loaded, 16)
            act.dma_start(VEC1[64:128, :], gate_bias.rearrange("a b (k p) -> (a b k) p", p=P)).then_inc(vec_loaded, 16)
            act.dma_start(VEC2[0:48, :], conv_w.rearrange("a b (k p) -> (a b k) p", p=P)).then_inc(vec_loaded, 16)
            act.dma_start(VEC2[48:49, :], hgrn_norm_w).then_inc(vec_loaded, 16)
            act.wait_ge(consts, EPS_WRITTEN)
            act.activation(ST[:, 19:20], EPT[:, :], ACT.Sqrt)
            for n in range(0, 2 * D // XC, 4):
                for half in range(2):
                    act.wait_ge(x_loaded[n + half], 16)
                    act.drain()
                    act.activation(SQA[:, :], XS[:, half, n // 2 * XC:(n // 2 + 1) * XC], ACT.Square,
                                   accum_out=ST[:, 4 * half + n // 4:4 * half + n // 4 + 1]).then_inc(x_sq, 1)
            act.wait_ge(x_var, 1)
            act.activation(ST[:, 10:12], ST[:, 8:10], ACT.Sqrt, bias=EPT[:, :], scale=1.0 / D).then_inc(x_std, 1)

            def hi(turn, s, free=True):
                act.wait_ge(raw_loaded[s], turn * 16 + 16)
                if free:
                    act.wait_ge(w_used, RING * turn + s - (RING - 1))
                act.activation(WS[s][:, :, 0:GW], RAW[s][:, :, :], ACT.Copy).then_inc(hi_ready, 1)

            def small_half(group, chunks, par, free=True):
                act.wait_ge(w_used, chunks)
                if free:
                    act.wait_ge(drained, group - 1)
                act.activation(SM[par][:, :, :], PS[par][:, :, T:2 * T], ACT.Copy).then_inc(small_out, 1)

            def norm_x(c):
                act.activation(XS[:, 1, c * XC:(c + 1) * XC], XS[:, 1, c * XC:(c + 1) * XC], ACT.Copy,
                               scale=ST[:, 13:14]).then_inc(x_norm_act, 1)

            hi(0, 0, free=False)
            act.wait_ge(x_rstd, 1)
            norm_x(1)
            hi(0, 1, free=False)
            act.wait_ge(vec_out, 1)
            for c in range(CD):
                for k in range(KC * c, KC * (c + 1)):
                    act.wait_ge(x_turned, k + 1)
                    act.activation(U[:, k, 0:T], XB[k % len(XB)], ACT.Copy, scale=NW[:, k:k + 1]).then_inc(u_hi, 1)
                if c < 2:
                    norm_x(c + 2)
                hi((c + 2) // RING, (c + 2) % RING, free=c >= 2)
            act.wait_ge(lb_shift, 1)
            act.activation(LT[:, 0:32], LT[:, 0:32], ACT.Exp).then_inc(lb_exp, 1)

            def attention(a, slot):
                if slot == 1:
                    act.wait_ge(drained, 4 * a + 4)
                    act.activation(SG[:, :], G[:, :], ACT.Sigmoid).then_inc(gate_g, 1)
                if slot == 11:
                    act.wait_ge(o_done, a + 1)
                    act.activation(O2[:, :], OB[:, :], ACT.Square).then_inc(o_out, 1)
                    act.activation(O[:, :], OB[:, :], ACT.Copy).then_inc(o_out, 1)
                if slot == 13:
                    act.wait_ge(ss_done, a + 1)
                    act.activation(RS[:, 0, :], SS[:, 0:4], ACT.Sqrt, bias=EPT[:, :],
                                   scale=1.0 / P).then_inc(std_ready, 1)

            def gates(i):
                for h in range(2):
                    one = bass.ds(i * 2 + h, 1)
                    act.activation(PRE[:, h * T:(h + 1) * T], SF[:, h * T:(h + 1) * T], ACT.Identity,
                                   scale=OMLB[:, one], bias=LB[:, one])
                act.drain()
                act.activation(K[:, :], PRE[:, :], ACT.Copy, scale=-1.0, bias=1.0).then_inc(gate_f, 1)

            def branch(i, turn0, group0, a=None, first=False, is_conv=False):
                for slot in range(SLOTS):
                    for c in (2 * slot, 2 * slot + 1):
                        if not (first and slot < EARLY):
                            hi(turn0 + TURNS_BRANCH * i + c // RING + 1, c % RING)
                    if a is not None:
                        attention(a, slot)
                    if slot == 5:
                        act.wait_ge(drained, group0 + 4 * i + 1)
                        op = act.activation(SF[:, :], F[:, :], ACT.Sigmoid)
                        if is_conv:
                            op.then_inc(gate_f, 1)
                    if slot == 14 and not is_conv:
                        act.drain()
                        if a is None:
                            act.wait_ge(lb_ready, 1)
                        else:
                            act.wait_ge(level_ready, 8 * a + 8)
                        gates(i)
                    if slot % 4 == 3:
                        n = slot // 4
                        small_half(group0 + 4 * i + n, RING * (turn0 + TURNS_BRANCH * i) + CD * (n + 1), n % 2, free=not (first and n < 2))

            branch(0, 0, 0, first=True)
            with act.Fori(1, NP) as i:
                branch(i, 0, 0, a=i - 1)
            branch(0, CONV_TURN, CONV_GROUP, a=NP - 1, is_conv=True)
            with act.Fori(1, NP) as i:
                branch(i, CONV_TURN, CONV_GROUP, is_conv=True)

            def merge(i, last=False):
                turn = MERGE_TURN + TURNS_MERGE * i + 1
                group = MERGE_GROUP + 4 * i
                chunks = RING * (MERGE_TURN + TURNS_MERGE * i)
                for c in range(2 * CD + 2 * CB):
                    hi(turn + c // RING, c % RING)
                    if c in (CD + 2, 2 * CD + 2):
                        n = c // CD - 1
                        act.wait_ge(drained, group + n + 1)
                        for t in range(2):
                            gate = (GA, GB)[n][:, t * T:(t + 1) * T]
                            act.activation(gate, gate, ACT.Sigmoid,
                                           bias=VT1[:, bass.ds(i * 2 + (64 + n * KT + t), 1)]).then_inc(merge_gate, 1)
                    if c == CD - 1:
                        small_half(group, chunks + c + 1, 0)
                    if c == 2 * CD - 1:
                        small_half(group + 1, chunks + c + 1, 1)
                    if last and c > 2 * CD:
                        split_merged(c - 2 * CD - 1)
                    if c == 2 * CD + CB - 1:
                        small_half(group + 2, chunks + c + 1, 0)
                    if c == 2 * CD + 2 * CB - 1:
                        small_half(group + 3, chunks + c + 1, 1)

            def split_merged(n):
                act.wait_ge(w_used, RING * OUT_TURN - 2 * CB)
                act.wait_ge(merged, 2 * n + 2)
                act.activation(U[:, KC * n:KC * (n + 1), 0:T], MRG[:, KC * n:KC * (n + 1), :], ACT.Copy).then_inc(m_hi, 1)

            with act.Fori(0, NG - 1) as i:
                merge(i)
            merge(NG - 1, last=True)
            split_merged(CD - 1)

            def output(i, last=False):
                for n in range(2):
                    for c in range(CD if not (last and n == 1) else RING):
                        hi(OUT_TURN + TURNS_OUT * i + (n * CD + c) // RING + 1, c % RING)
                    if last and n == 1:
                        act.activation(ST[:, 19:20], EPT[:, :], ACT.Sqrt)
                    small_half(OUT_GROUP + 2 * i + n, RING * (OUT_TURN + TURNS_OUT * i) + CD * (n + 1), n)
                    act.wait_ge(h_ready, 2 * i + n + 1)
                    for b in range(2):
                        act.activation(SM[n][:, b, :], (GA, GB)[n][:, b * T:(b + 1) * T], ACT.Square,
                                       accum_out=SSQ[:, b, bass.ds(i * 2 + n, 1)]).then_inc(h_sq, 1)

            with act.Fori(0, NG // 2 - 1) as i:
                output(i)
            output(NG // 2 - 1, last=True)
            act.wait_ge(tail_var, 1)
            act.activation(ST[:, 10:12], ST[:, 8:10], ACT.Sqrt, bias=EPT[:, :], scale=1.0 / D).then_inc(tail_std, 1)
            act.wait_ge(tail_rstd, 1)
            for half, c, done, _ in OUT_PIECES:
                if done is out_act:
                    piece = H[:, half, c * XC:(c + 1) * XC]
                    act.activation(piece, piece, ACT.Copy, scale=ST[:, 12 + half:13 + half]).then_inc(out_act, 1)

        @block.vector
        def _(dve):
            def after():
                dve.drain()

            def rstd(r, std, var, tmp):
                dve.reciprocal(r, std)
                after()
                dve.tensor_tensor(tmp, r, r, ALU.mult)
                after()
                dve.tensor_tensor(tmp, tmp, var, ALU.mult)
                after()
                dve.tensor_scalar(tmp, tmp, -0.5, 1.5, ALU.mult, ALU.add)
                after()
                return dve.tensor_tensor(r, r, tmp, ALU.mult)

            for n in range(2, 2 * D // XC, 4):
                for half in range(2):
                    piece = XS[:, half, n // 2 * XC:(n // 2 + 1) * XC]
                    col = 4 * half + 2 + n // 4
                    dve.wait_ge(x_loaded[n + half], 16)
                    after()
                    dve.tensor_tensor_reduce(out=SQD[:, :], in0=piece, in1=piece, scale=1.0, scalar=0.0,
                                             op0=ALU.mult, op1=ALU.add, accum_out=ST[:, col:col + 1])
            after()
            dve.wait_ge(x_sq, 4)
            dve.tensor_reduce(ST[:, 8:10], ST[:, 0:8].rearrange("p (b n) -> p b n", b=2), AX.X, ALU.add).then_inc(x_var, 1)
            after()
            dve.tensor_scalar(ST[:, 14:16], ST[:, 8:10], 1.0 / D, EPS, ALU.mult, ALU.add)
            dve.wait_ge(vec_turned, 1)
            dve.tensor_copy(VT1[:, :], SC[0][:, 0:P])
            dve.tensor_copy(VT2[:, :], SC[0][:, P:P + 49]).then_inc(vec_out, 1)
            dve.wait_ge(x_std, 1)
            after()
            rstd(ST[:, 12:14], ST[:, 10:12], ST[:, 14:16], ST[:, 16:18]).then_inc(x_rstd, 1)
            after()

            def norm_x(half, c):
                dve.tensor_scalar(XS[:, half, c * XC:(c + 1) * XC], XS[:, half, c * XC:(c + 1) * XC],
                                  ST[:, 12 + half:13 + half], None, ALU.mult).then_inc(x_norm_dve, 1)

            def lo(turn, s):
                dve.wait_ge(hi_ready, RING * turn + s + 1)
                dve.tensor_tensor(WS[s][:, :, GW:2 * GW], RAW[s][:, :, :], WS[s][:, :, 0:GW],
                                  ALU.subtract).then_inc(lo_ready, 1)

            norm_x(0, 0)
            norm_x(1, 0)
            norm_x(0, 1)
            lo(0, 0)
            norm_x(0, 2)
            norm_x(0, 3)
            lo(0, 1)
            for c in range(CD):
                for k in range(KC * c, KC * (c + 1)):
                    dve.wait_ge(u_hi, k + 1)
                    dve.scalar_tensor_tensor(U[:, k, T:2 * T], XB[k % len(XB)], NW[:, k:k + 1], U[:, k, 0:T],
                                             ALU.mult, ALU.subtract).then_inc(u_ready, 1)
                lo((c + 2) // RING, (c + 2) % RING)
            dve.tensor_tensor(LT[:, 32:48], VT1[:, 32:48], VT1[:, 48:64], ALU.max)
            after()
            dve.tensor_tensor(LT[:, 0:16], VT1[:, 32:48], LT[:, 32:48], ALU.subtract)
            dve.tensor_tensor(LT[:, 16:32], VT1[:, 48:64], LT[:, 32:48], ALU.subtract).then_inc(lb_shift, 1)
            dve.wait_ge(consts, N_CONSTS)
            dve.wait_ge(lb_exp, 1)
            dve.tensor_tensor(LT[:, 32:48], LT[:, 0:16], LT[:, 16:32], ALU.add)
            after()
            dve.reciprocal(LT[:, 32:48], LT[:, 32:48])
            after()
            dve.tensor_tensor(LB[:, :], LT[:, 0:16], LT[:, 32:48], ALU.mult)
            after()
            dve.tensor_scalar(OMLB[:, :], LB[:, :], -1.0, 1.0, ALU.mult, ALU.add).then_inc(lb_ready, 1)

            def drain_group(dst, group, par):
                dve.wait_ge(small_out, group + 1)
                dve.tensor_tensor(dst, PS[par][:, :, 0:T], SM[par][:, :, :], ALU.add).then_inc(drained, 1)

            def pair(t):
                return t[:, :].rearrange("p (t n) -> p t n", t=2)

            def store_y(y, kt):
                ys = Y[:, bass.ds(kt, 2), :]
                dve.tensor_copy(ys[:, :, 0:T], y)
                after()
                dve.tensor_tensor(ys[:, :, T:2 * T], y, ys[:, :, 0:T], ALU.subtract).then_inc(y_ready, 1)

            def halves(t, m):
                v = t.rearrange("p (n two m) -> p n two m", two=2, m=m)
                return v[:, :, 0, :], v[:, :, 1, :]

            def produce(n):
                m = LEVELS[n]
                blocks = W2 // (2 * m)
                qr = QR[:, n % 2, :].rearrange("p (n m) -> p n m", m=m)
                q_right = halves(Q[:, :], m)[1]
                p_left, p_right = halves(PRE[:, :], m)
                s_left, s_right = halves(SUF[:, :], m)
                op = dve.tensor_tensor(qr, q_right, p_right, ALU.mult)
                if m > 1:
                    op = dve.tensor_tensor(halves(KL[:, n % 2, :], m)[0], halves(K[:, :], m)[0], s_left, ALU.mult)
                op.then_inc(level_ready, 1)
                if m == T // 2:
                    return
                over_right = p_right[:, :, m - 1:m].broadcast_to([P, blocks, m])
                over_left = p_left[:, :, m - 1:m].broadcast_to([P, blocks, m])
                if m == 1:
                    dve.memset(s_right, 1.0)
                    dve.tensor_copy(s_left, over_right)
                else:
                    dve.tensor_tensor(s_left, s_left, over_right, ALU.mult)
                after()
                dve.tensor_tensor(p_right, p_right, over_left, ALU.mult)
                after()

            def consume(a, n):
                m = LEVELS[n]
                if m == P:
                    dve.tensor_copy(AO[:, :, :], SC[n % 2][:, 0:T].rearrange("p (h t) -> p h t", h=2)).then_inc(level_read, 1)
                    return
                if n == 0:
                    eye = IDN[:, :].bitcast(U32).unsqueeze(1).broadcast_to([P, 4, P])
                    dve.copy_predicated(AD[:, :, :], eye, SS[:, :].rearrange("p (g t) -> p g t", g=4))
                after()
                dst = AD[:, :, :].rearrange("p g (j two r) -> p g j two r", two=2, r=m)[:, :, :, 1, :]
                data = SC[n % 2][:, 0:T].rearrange("p (g j r) -> p g j r", g=4, r=m)
                mask = MASK[:, n * 64:(n + 1) * 64].bitcast(U32).rearrange("p (j r) -> p j r", r=m)
                mask = mask.unsqueeze(1).broadcast_to([P, 4, 64 // m, m])
                dve.copy_predicated(dst, mask, data).then_inc(level_read, 1)

            def attention(a, slot):
                if slot == 0:
                    dve.wait_ge(gate_f, a + 1)
                if 2 <= slot < 10:
                    consume(a, slot - 2)
                if slot < 8:
                    produce(slot)
                if slot == 14:
                    dve.wait_ge(std_ready, a + 1)
                    dve.tensor_scalar(RS[:, 1, :], SS[:, 0:4], 1.0 / P, EPS, ALU.mult, ALU.add)
                    after()
                    rstd(RS[:, 2, :], RS[:, 0, :], RS[:, 1, :], RS[:, 3, :])
                    after()
                    for g in range(4):
                        op = dve.tensor_scalar(GA[:, g * P:(g + 1) * P], IDN[:, :], RS[:, 2, g:g + 1], None, ALU.mult)
                    op.then_inc(rstd_ready, 1)
                if slot == 15:
                    dve.wait_ge(o_out, 2 * a + 2)
                    dve.wait_ge(gate_g, a + 1)
                    dve.wait_ge(rstd_spread, a + 1)
                    dve.scalar_tensor_tensor(O[:, :], O[:, :], HW0, SS[:, :], ALU.mult, ALU.mult)
                    dve.tensor_tensor(SG[:, :], SG[:, :], G[:, :], ALU.mult)
                    after()
                    dve.tensor_tensor(O[:, :], O[:, :], SG[:, :], ALU.mult)
                    after()
                    store_y(pair(O), a * 2)

            def conv(i, slot):
                if slot == 8:
                    dve.wait_ge(gate_f, NP + i + 1)
                    dve.tensor_tensor(SF[:, :], SF[:, :], F[:, :], ALU.mult)
                if slot == 12:
                    dve.memset(UP[:, :, 0:2], 0.0)
                    dve.tensor_tensor(UP[:, :, 2:T + 2], pair(Q), pair(V), ALU.mult)
                    after()
                if slot == 13:
                    for j in range(3):
                        for t in range(2):
                            tap = VT2[:, bass.ds(i * 2 + (16 * j + t), 1)]
                            acc = K[:, t * T:(t + 1) * T]
                            if j == 0:
                                dve.tensor_scalar(acc, UP[:, t, j:T + j], tap, None, ALU.mult)
                            else:
                                dve.scalar_tensor_tensor(acc, UP[:, t, j:T + j], tap, acc, ALU.mult, ALU.add)
                        after()

            def branch(i, turn0, group0, a=None, first=False, is_conv=False):
                for slot in range(SLOTS):
                    for c in (2 * slot, 2 * slot + 1):
                        if a is not None and c == 2 * slot + 1 and 2 <= slot < 10:
                            dve.wait_ge(level_done, 8 * a + slot - 1)
                        if not (first and slot < EARLY):
                            lo(turn0 + TURNS_BRANCH * i + c // RING + 1, c % RING)
                    if a is not None:
                        attention(a, slot)
                    if is_conv:
                        conv(i, slot)
                    if slot % 4 == 3:
                        n = slot // 4
                        after()
                        if n == 2 and a is not None:
                            dve.wait_ge(o_done, a + 1)
                        drain_group(pair((F, Q, V, G)[n]), group0 + 4 * i + n, n % 2)
                        after()
                if is_conv:
                    dve.tensor_tensor(K[:, :], K[:, :], G[:, :], ALU.mult)
                    after()
                    dve.tensor_tensor(K[:, :], K[:, :], SF[:, :], ALU.mult)
                    after()
                    store_y(pair(K), i * 2 + KB)
                    after()

            branch(0, 0, 0, first=True)
            with dve.Fori(1, NP) as i:
                branch(i, 0, 0, a=i - 1)
            branch(0, CONV_TURN, CONV_GROUP, a=NP - 1, is_conv=True)
            with dve.Fori(1, NP) as i:
                branch(i, CONV_TURN, CONV_GROUP, is_conv=True)

            def split_merged(n):
                dve.wait_ge(m_hi, n + 1)
                k = slice(KC * n, KC * (n + 1))
                dve.tensor_tensor(U[:, k, T:2 * T], MRG[:, k, :], U[:, k, 0:T], ALU.subtract).then_inc(m_ready, 1)

            def merge(i, last=False):
                turn = MERGE_TURN + TURNS_MERGE * i + 1
                group = MERGE_GROUP + 4 * i
                out2 = MRG[:, bass.ds(i * 2, 2), :]
                for c in range(2 * CD + 2 * CB):
                    lo(turn + c // RING, c % RING)
                    if c == CD - 1:
                        drain_group(pair(GA), group, 0)
                    if c == 2 * CD - 1:
                        drain_group(pair(GB), group + 1, 1)
                    if last and c > 2 * CD:
                        split_merged(c - 2 * CD - 1)
                    if c == 2 * CD + CB - 1:
                        drain_group(pair(Z), group + 2, 0)
                        after()
                        dve.wait_ge(merge_gate, 4 * i + 2)
                        dve.tensor_tensor(out2, pair(GA), pair(Z), ALU.mult)
                        after()
                drain_group(pair(Z), group + 3, 1)
                after()
                dve.wait_ge(merge_gate, 4 * i + 4)
                dve.tensor_tensor(Z[:, :], GB[:, :], Z[:, :], ALU.mult)
                after()
                dve.tensor_tensor(out2, out2, pair(Z), ALU.add).then_inc(merged, 1)
                after()

            with dve.Fori(0, NG - 1) as i:
                merge(i)
            merge(NG - 1, last=True)
            split_merged(CD - 1)

            def output(i, first=False, last=False):
                for n in range(2):
                    for c in range(CD if not (last and n == 1) else RING):
                        lo(OUT_TURN + TURNS_OUT * i + (n * CD + c) // RING + 1, c % RING)
                    h = pair((GA, GB)[n])
                    if not first:
                        dve.wait_ge(h_sq, 4 * i + 2 * n - 2)
                    drain_group(h, OUT_GROUP + 2 * i + n, n)
                    after()
                    cols = bass.ds(i * 2 * GW + n * GW, GW)
                    dve.wait_ge(xr_loaded[n], i * 32 + 32)
                    dve.tensor_tensor(h, h, XR[:, :, cols], ALU.add).then_inc(h_ready, 1)
                    after()
                    fw = FW[:, cols].unsqueeze(1).broadcast_to([P, 2, GW])
                    dve.tensor_tensor(H[:, :, cols], h, fw, ALU.mult)

            output(0, first=True)
            with dve.Fori(1, NG // 2 - 1) as i:
                output(i)
            output(NG // 2 - 1, last=True)
            dve.wait_ge(h_sq, 2 * NG)
            dve.tensor_reduce(ST[:, 8:10], SSQ[:, :, :], AX.X, ALU.add).then_inc(tail_var, 1)
            after()
            dve.tensor_scalar(ST[:, 14:16], ST[:, 8:10], 1.0 / D, EPS, ALU.mult, ALU.add)
            dve.wait_ge(tail_std, 1)
            after()
            rstd(ST[:, 12:14], ST[:, 10:12], ST[:, 14:16], ST[:, 16:18]).then_inc(tail_rstd, 1)
            after()
            for half, c, done, _ in OUT_PIECES:
                if done is out_dve:
                    piece = H[:, half, c * XC:(c + 1) * XC]
                    dve.tensor_scalar(piece, piece, ST[:, 12 + half:13 + half], None, ALU.mult).then_inc(out_dve, 1)

        @block.tensor
        def _(pe):
            pe.wait_ge(consts, IDN_WRITTEN)
            pe.wait_ge(vec_loaded, 80)
            pe.transpose(SC[0][:, 0:P], VEC1[:, :], IDN[:, :])
            pe.transpose(SC[0][:, P:P + 49], VEC2[0:49, :], IDN[0:49, 0:49]).then_inc(vec_turned, 1)
            pe.wait_ge(vec_out, 1)

            def turn_x(k):
                pe.wait_ge(x_norm_dve, k * P // XC + 2)
                pe.wait_ge(x_norm_act, k * P // XC)
                if k >= len(XB):
                    pe.wait_ge(u_ready, k - len(XB) + 1)
                for b in range(2):
                    op = pe.transpose(XB[k % len(XB)][:, b * P:(b + 1) * P], XS[:, b, k * P:(k + 1) * P], IDN[:, :])
                op.then_inc(x_turned, 1)

            for k in range(len(XB)):
                turn_x(k)

            def split_product(bank, stat_hi, stat_lo, both, first, last):
                def with_lo(stop):
                    return pe.matmul(bank[:, T:2 * T], stat_lo, both[:, 0:T], start=False, stop=stop,
                                     skip_group_check=True)

                if not first:
                    with_lo(False)
                op = pe.matmul(bank, stat_hi, both, start=first, stop=last, skip_group_check=True)
                return with_lo(False) if first else op

            def channels(par, s, rhs, k0, n_tiles):
                for k in range(KC):
                    for t in range(2):
                        op = split_product(PS[par][:, t, :], WS[s][:, k, t * P:(t + 1) * P],
                                           WS[s][:, k, GW + t * P:GW + (t + 1) * P], rhs[:, k0 + k, :],
                                           k0 + k == 0, k0 + k == n_tiles - 1)
                return op

            def positions(par, s, lhs, k0, n_tiles):
                for k in range(KC):
                    for b in range(2):
                        op = split_product(PS[par][:, b, :], lhs[:, k0 + k, b * P:(b + 1) * P],
                                           lhs[:, k0 + k, T + b * P:T + (b + 1) * P], WS[s][:, k, :],
                                           k0 + k == 0, k0 + k == n_tiles - 1)
                return op

            def attention(a, c):
                if c % 2 == 0 and 4 <= c < 20:
                    n = (c - 4) // 2
                    pe.wait_ge(level_ready, 8 * a + (n + 1))
                    if n >= 2:
                        pe.wait_ge(level_read, 8 * a + (n - 1))
                    if n == 7:
                        for h in range(2):
                            op = pe.matmul(SC[n % 2][:, h * P:(h + 1) * P], KL[:, n % 2, h * T:h * T + P],
                                           QR[:, n % 2, h * P:(h + 1) * P], start=True, stop=True)
                    else:
                        for g in range(4):
                            k_side = (K[:, :] if n == 0 else KL[:, n % 2, :])[:, g * P:(g + 1) * P]
                            op = pe.matmul(SC[n % 2][:, g * 64:(g + 1) * 64], k_side,
                                           QR[:, n % 2, g * 64:(g + 1) * 64], start=True, stop=True)
                            if n == 0:
                                op = pe.matmul(SS[:, g * P:(g + 1) * P], k_side, Q[:, g * P:(g + 1) * P],
                                               start=True, stop=True)
                    op.then_inc(level_done, 1)
                if c == 22:
                    pe.wait_ge(level_read, 8 * a + 8)
                    for h in range(2):
                        v = [V[:, b * T + h * P:b * T + (h + 1) * P] for b in range(2)]
                        pe.matmul(OB[:, h * T:h * T + P], v[0], AD[:, 2 * h, :], start=True, stop=True)
                        pe.matmul(OB[:, h * T + P:(h + 1) * T], v[0], AO[:, h, :], start=True, stop=False)
                        op = pe.matmul(OB[:, h * T + P:(h + 1) * T], v[1], AD[:, 2 * h + 1, :], start=False, stop=True)
                    op.then_inc(o_done, 1)
                if c == 26:
                    pe.wait_ge(o_out, 2 * a + 1)
                    for g in range(4):
                        op = pe.matmul(SS[:, g:g + 1], O2[:, g * P:(g + 1) * P], ONES[:, 0:1], start=True, stop=True)
                    op.then_inc(ss_done, 1)
                if c == 31:
                    pe.wait_ge(rstd_ready, a + 1)
                    pe.matmul(SS[:, :], ONES[:, :], GA[:, :], start=True, stop=True).then_inc(rstd_spread, 1)

            def group(turn, n0, n_chunks, mode, operand, k_start, par, gidx, free=True, u_wait=None, a=None):
                if free:
                    pe.wait_ge(drained, gidx - 1)
                for c in range(n_chunks):
                    if u_wait is not None and u_wait[0] is u_ready:
                        for k in range(max(KC * (c + 1), len(XB)), min(KC * (c + 2), KT)):
                            turn_x(k)
                    if u_wait is not None:
                        pe.wait_ge(u_wait[0], u_wait[1] * (c + 1))
                    at_chunk = n0 + c
                    pe.wait_ge(lo_ready, RING * (turn + at_chunk // RING) + at_chunk % RING + 1)
                    op = mode(par, at_chunk % RING, operand[:, k_start:k_start + n_chunks * KC, :], c * KC,
                              n_chunks * KC)
                    op.then_inc(w_used, 1)
                    if a is not None:
                        attention(a, at_chunk)

            def branch(i, turn0, group0, modes, a=None, first=False):
                for n in range(4):
                    group(turn0 + TURNS_BRANCH * i, n * CD, CD, modes[n], U, 0, n % 2, group0 + 4 * i + n,
                          free=not (first and n < 2), u_wait=(u_ready, KC) if first and n == 0 else None, a=a)

            hgrn = (channels, channels, positions, channels)
            branch(0, 0, 0, hgrn, first=True)
            with pe.Fori(1, NP) as i:
                branch(i, 0, 0, hgrn, a=i - 1)
            branch(0, CONV_TURN, CONV_GROUP, (channels,) * 4, a=NP - 1)
            with pe.Fori(1, NP) as i:
                branch(i, CONV_TURN, CONV_GROUP, (channels,) * 4)
            with pe.Fori(0, NG) as i:
                turn, g = MERGE_TURN + TURNS_MERGE * i, MERGE_GROUP + 4 * i
                group(turn, 0, CD, channels, U, 0, 0, g)
                group(turn, CD, CD, channels, U, 0, 1, g + 1)
                pe.wait_ge(y_ready, 2 * NP)
                group(turn, 2 * CD, CB, channels, Y, 0, 0, g + 2)
                group(turn, 2 * CD + CB, CB, channels, Y, KB, 1, g + 3)

            def output(i, first=False):
                for n in range(2):
                    group(OUT_TURN + TURNS_OUT * i, n * CD, CD, positions, U, 0, n, OUT_GROUP + 2 * i + n,
                          u_wait=(m_ready, 1) if first and n == 0 else None)

            output(0, first=True)
            with pe.Fori(1, NG // 2) as i:
                output(i)


_INS = ["x", "norm_w", "w_in", "lb_logits", "hgrn_norm_w", "conv_w", "w_branch_a", "w_branch_b",
        "gate_bias", "w_out", "final_norm_w"]


def kernel(**inputs):
    import numpy as np
    import concourse.bacc as bacc
    from concourse import mybir as mb
    from concourse.bass_utils import run_bass_kernel_spmd

    nc = bacc.Bacc("TRN2", target_bir_lowering=False, num_devices=1, dynamic_dma_scratch_size=1024)
    arrays, args = {}, []
    for name in _INS:
        a = np.ascontiguousarray(inputs[name])
        arrays[f"in_{name}"] = a
        args.append(nc.dram_tensor(f"in_{name}", a.shape, mb.dt.from_np(a.dtype), kind="ExternalInput").ap())
    out = nc.dram_tensor("out_dram", (1, T, D), F32, kind="ExternalOutput").ap()
    build(nc, *args, out)
    r = run_bass_kernel_spmd(nc, [arrays], core_ids=[0])
    return r.results[0]["out_dram"]
```

```python
import concourse.bass as bass
from concourse import mybir
from contextlib import ExitStack

F32 = mybir.dt.float32
F32R = mybir.dt.float32r
U32 = mybir.dt.uint32
ALU = mybir.AluOpType
ACT = mybir.ActivationFunctionType
AX = mybir.AxisListType

P = 128
T = 256
D = 4096
KT = D // P
BW = 2048
KB = BW // P
GW = 256
KC = 4
RING = 4
CD, CB = KT // KC, KB // KC
NP = BW // GW
NG = D // GW
XW = KC * P
XC = 1024
EARLY = 2
SLOTS = 16
LEVELS = (1, 2, 4, 8, 16, 32, 64, 128)
EPS = 1e-6
A_Q, A_F, A_I, A_G, C_B, C_C, C_H, C_G = (BW * n for n in range(8))
G_A, G_B = 8 * BW, 8 * BW + D
HGRN_GROUPS = (A_F, A_Q, A_I, A_G)
CONV_GROUPS = (C_G, C_C, C_H, C_B)
X_AHEAD = ((4, 5), (6,), (7,), ())
TURNS_BRANCH = 4 * CD // RING
TURNS_MERGE = (2 * CD + 2 * CB) // RING
TURNS_OUT = 2 * CD // RING
CONV_TURN = NP * TURNS_BRANCH
MERGE_TURN = 2 * CONV_TURN
OUT_TURN = MERGE_TURN + NG * TURNS_MERGE
CONV_GROUP = 4 * NP
MERGE_GROUP = 2 * CONV_GROUP
OUT_GROUP = MERGE_GROUP + 4 * NG


def build(nc, x, norm_w, w_in, lb_logits, hgrn_norm_w, conv_w, w_branch_a, w_branch_b,
          gate_bias, w_out, final_norm_w, out):
    ctx = ExitStack()
    with ctx:
        def sb(name, shape, dt=F32):
            return ctx.enter_context(nc.sbuf_tensor(name, shape, dt))

        def at(name, shape, offset, dt=F32):
            return nc.alloc_sbuf_tensor_at(name, shape, dt, offset=offset)

        def sem(name):
            return ctx.enter_context(nc.semaphore(name))

        base = (nc.sbuf_base + 31) // 32 * 32
        region_u = base
        region_y = region_u + KT * 2 * T * 4
        region_m = region_y + 2 * KB * 2 * T * 4
        region_end = region_m + KT * T * 4
        ctx.enter_context(nc.sbuf_tensor("arena", [P, (region_end - nc.sbuf_base + 3) // 4], F32))
        U = at("U", [P, KT, 2 * T], region_u, F32R)
        Y = at("Y", [P, 2 * KB, 2 * T], region_y, F32R)
        XS = at("XS", [P, 2, D], region_y)
        H = at("H", [P, 2, D], region_y)
        XR = at("XR", [P, 2, D], region_y + 2 * D * 4)
        MRG = at("MRG", [P, KT, T], region_m)
        FW = at("FW", [P, D], region_m)
        SQA = at("SQA", [P, XW], region_m)
        SQD = at("SQD", [P, XW], region_m + 4 * XW)
        VEC1 = at("VEC1", [P, P], region_m + 8 * XW)
        VEC2 = at("VEC2", [P, P], region_m + 8 * XW + 4 * P)
        ONES = at("ONES", [P, P], region_m + 8 * XW + 8 * P)
        VEC0 = at("VEC0", [KT, P], region_m + 8 * XW + 12 * P)
        W2 = 2 * T
        names = ["F", "V", "G", "SF", "SG", "PRE", "K", "SUF"]
        F, V, G, SF, SG, PRE, K, SUF = [at(n, [P, W2], region_m + 4 * W2 * i)
                                        for i, n in enumerate(names)]
        QX = at("QX", [P, 4, 192], region_m + 4 * W2 * len(names))
        QC = at("QC", [P, W2], region_m + 4 * W2 * len(names))
        scr = region_m + 4 * W2 * len(names) + 16 * 192
        KL = at("KL", [P, 2, W2], scr)
        UP = at("UP", [P, 2, T + 2], scr)
        QR = at("QR", [P, 2, T], scr + 16 * T)
        AD = at("AD", [P, 4, P], scr + 24 * T)
        AO = at("AO", [P, 2, P], scr + 32 * T)
        O = at("O", [P, W2], scr + 36 * T)
        O2 = at("O2", [P, W2], scr + 44 * T)
        RAW = [sb(f"RAW{i}", [P, KC, GW]) for i in range(RING)]
        WS = [sb(f"WS{i}", [P, KC, 2 * GW], F32R) for i in range(RING)]
        SM = [sb(f"SM{i}", [P, 2, T]) for i in range(2)]
        GA, GB, Z = [sb(n, [P, W2]) for n in ("GA", "GB", "Z")]
        MASK = sb("MASK", [P, 6 * 64])
        IDN = sb("IDN", [P, P])
        RB = sb("RB", [P, T])
        NW = sb("NW", [P, KT])
        VT1 = sb("VT1", [P, 96])
        VT2 = sb("VT2", [P, 49])
        LB = sb("LB", [P, 16])
        OMLB = sb("OMLB", [P, 16])
        LT = sb("LT", [P, 48])
        SSQ = sb("SSQ", [P, 2, NG])
        ST = sb("ST", [P, 20])
        RS = sb("RS", [P, 5, 4])
        EPT = sb("EPT", [P, 1])
        HW0 = VT2[:, 48:49]

        PS = [ctx.enter_context(nc.psum_tensor(f"PS{i}", [P, 2, 512], F32)) for i in range(2)]
        SC = [ctx.enter_context(nc.psum_tensor(f"SC{i}", [P, 512], F32)) for i in range(2)]
        OB = ctx.enter_context(nc.psum_tensor("OB", [P, 512], F32))
        SS = ctx.enter_context(nc.psum_tensor("SS", [P, 512], F32))

        XB = [b[:, 0:T] for b in (PS[1][:, 0, :], PS[1][:, 1, :], SC[0], SC[1], OB, SS)]

        EPS_WRITTEN, IDN_WRITTEN, N_CONSTS = 1, 3, 19

        raw_loaded = [sem(f"raw_loaded{i}") for i in range(RING)]
        hi_ready = sem("hi_ready")
        lo_ready = sem("lo_ready")
        w_used = sem("w_used")
        small_out = sem("small_out")
        drained = sem("drained")
        x_loaded = [sem(f"x_loaded{i}") for i in range(CD)]
        gain_loaded = sem("gain_loaded")
        gain_turned = sem("gain_turned")
        gain_out = sem("gain_out")
        vec_loaded = sem("vec_loaded")
        consts = sem("consts")
        x_sq = sem("x_sq")
        x_var = sem("x_var")
        x_std = sem("x_std")
        x_rstd = sem("x_rstd")
        x_spread = sem("x_spread")
        vec_turned = sem("vec_turned")
        lb_shift = sem("lb_shift")
        lb_exp = sem("lb_exp")
        lb_ready = sem("lb_ready")
        x_turned = sem("x_turned")
        u_hi = sem("u_hi")
        u_ready = sem("u_ready")
        gate_f = sem("gate_f")
        gate_g = sem("gate_g")
        level_ready = sem("level_ready")
        level_done = sem("level_done")
        level_read = sem("level_read")
        o_done = sem("o_done")
        std_ready = sem("std_ready")
        o_ready = sem("o_ready")
        o_turned = sem("o_turned")
        y_ready = sem("y_ready")
        merge_gate = sem("merge_gate")
        merged = sem("merged")
        m_hi = sem("m_hi")
        m_ready = sem("m_ready")
        xr_loaded = [sem(f"xr_loaded{i}") for i in range(2)]
        h_ready = sem("h_ready")
        h_sq = sem("h_sq")
        half_summed = sem("half_summed")
        tail_var = sem("tail_var")
        tail_std = sem("tail_std")
        tail_rstd = sem("tail_rstd")
        out_dve = sem("out_dve")
        out_act = sem("out_act")
        stored = sem("stored")

        OUT_PIECES = [(0, 0, out_dve, 1), (0, 1, out_act, 1), (0, 2, out_dve, 2), (0, 3, out_act, 2),
                      (1, 0, out_dve, 3), (1, 1, out_act, 3), (1, 2, out_dve, 4), (1, 3, out_act, 4)]

        block = ctx.enter_context(nc.Block())

        @block.sync
        def _(sp):
            sp.dma_start(VEC0[:, :], norm_w.rearrange("a (k p) -> (a k) p", p=P)).then_inc(gain_loaded, 16)

            def load_x(j):
                cols = slice(j * XW, (j + 1) * XW)
                sp.dma_start(XS[:, :, cols], x[0, :, cols].rearrange("(b p) c -> p b c", p=P)).then_inc(x_loaded[j], 16)

            def load(w, rows, col, turn, s, free=True):
                src = w[rows * KC * P:(rows + 1) * KC * P, bass.ds(col, GW)]
                if free:
                    sp.wait_ge(lo_ready, RING * turn + s - (RING - 1))
                sp.dma_start(RAW[s][:, :, :], src.rearrange("(k p) c -> p k c", p=P)).then_inc(raw_loaded[s], 16)

            def column(i, col):
                return i * GW + col if col else (i + 1) * GW - GW

            def load_vectors():
                sp.dma_start(VEC1[0:32, :], lb_logits.rearrange("a (k p) -> (a k) p", p=P)).then_inc(vec_loaded, 16)
                sp.dma_start(VEC1[32:96, :], gate_bias.rearrange("a b (k p) -> (a b k) p", p=P)).then_inc(vec_loaded, 16)
                sp.dma_start(VEC2[0:48, :], conv_w.rearrange("a b (k p) -> (a b k) p", p=P)).then_inc(vec_loaded, 16)
                sp.dma_start(VEC2[48:49, :], hgrn_norm_w).then_inc(vec_loaded, 16)

            def branch(i, cols, turn0, first=False):
                for n, col in enumerate(cols):
                    col = column(i, col)
                    for c in range(CD):
                        if first and n == 0:
                            for j in ((c,) if c < RING else X_AHEAD[c - RING]):
                                load_x(j)
                            if c == CD - 1:
                                load_vectors()
                        load(w_in[0], c, col, turn0 + TURNS_BRANCH * i + (n * CD + c) // RING, c % RING,
                             free=not (first and n == 0 and c < RING))

            branch(0, HGRN_GROUPS, 0, first=True)
            with sp.Fori(1, NP) as i:
                branch(i, HGRN_GROUPS, 0)
            with sp.Fori(0, NP) as i:
                branch(i, CONV_GROUPS, CONV_TURN)
            with sp.Fori(0, NG) as i:
                turn = MERGE_TURN + TURNS_MERGE * i
                for n, col in enumerate((G_A, G_B)):
                    col = column(i, col)
                    for c in range(CD):
                        load(w_in[0], c, col, turn + (n * CD + c) // RING, c % RING)
                col = column(i, 0)
                for n, w in enumerate((w_branch_a, w_branch_b)):
                    for c in range(CB):
                        load(w[0], c, col, turn + (2 * CD + n * CB + c) // RING, c % RING)
            with sp.Fori(0, NG // 2) as i:
                for n in range(2):
                    col = column(i * 2 + n, 0)
                    for c in range(CD):
                        load(w_out[0], c, col, OUT_TURN + TURNS_OUT * i + (n * CD + c) // RING, c % RING)
                    if n == 0:
                        sp.wait_ge(w_used, RING * OUT_TURN)
                        sp.wait_ge(m_ready, CD)
                    cols = bass.ds(col, GW)
                    sp.dma_start(XR[:, :, cols], x[0, :, cols].rearrange("(b p) c -> p b c", p=P)).then_inc(xr_loaded[n], 16)
                    sp.dma_start(FW[:, cols], final_norm_w[cols].partition_broadcast(P)).then_inc(xr_loaded[n], 16)
            for half, c, done, count in OUT_PIECES:
                sp.wait_ge(done, count)
                cols = slice(c * XC, (c + 1) * XC)
                sp.dma_start(out[0, half * P:(half + 1) * P, cols], H[:, half, cols]).then_inc(stored, 16)
            sp.wait_ge(stored, 16 * len(OUT_PIECES))

        @block.gpsimd
        def _(pool):
            pool.memset(EPT[:, :], EPS).then_inc(consts, 1)
            pool.memset(IDN[:, :], 0.0).then_inc(consts, 1)
            pool.wait_ge(consts, 2)
            pool.affine_select(out=IDN[:, :], in_=IDN[:, :], compare_op=ALU.not_equal, fill=1.0, base=0,
                               pattern=[[-1, P]], channel_multiplier=1).then_inc(consts, 1)
            pool.memset(MASK[:, :], 1.0).then_inc(consts, 1)
            pool.memset(ONES[:, :], 1.0).then_inc(consts, 1)
            pool.memset(AD[:, :, :], 0.0).then_inc(consts, 1)
            pool.memset(KL[:, :, :], 0.0).then_inc(consts, 1)
            pool.wait_ge(consts, 7)
            for n, m in enumerate(LEVELS[:6]):
                v = MASK[:, n * 64:(n + 1) * 64].rearrange("p (j r) -> p j r", r=m)
                pool.affine_select(out=v, in_=v, compare_op=ALU.is_ge, fill=0.0, base=0,
                                   pattern=[[-2 * m, 64 // m], [0, m]], channel_multiplier=1).then_inc(consts, 1)
                pool.wait_ge(consts, 8 + 2 * n)
                pool.affine_select(out=v, in_=v, compare_op=ALU.is_ge, fill=0.0, base=m - 1,
                                   pattern=[[2 * m, 64 // m], [0, m]], channel_multiplier=-1).then_inc(consts, 1)


        @block.scalar
        def _(act):
            act.wait_ge(consts, EPS_WRITTEN)
            act.activation(ST[:, 19:20], EPT[:, :], ACT.Sqrt)

            def hi(turn, s, free=True):
                act.wait_ge(raw_loaded[s], turn * 16 + 16)
                if free:
                    act.wait_ge(w_used, RING * turn + s - (RING - 1))
                act.activation(WS[s][:, :, 0:GW], RAW[s][:, :, :], ACT.Copy).then_inc(hi_ready, 1)

            def small_half(group, chunks, par, free=True, positions=False):
                act.wait_ge(w_used, chunks)
                if free:
                    act.wait_ge(drained, group - 1)
                if positions:
                    for b in range(2):
                        op = act.activation(SM[par][:, b, :], PS[par][:, b, T:2 * T], ACT.Copy, scale=ST[:, 12 + b:13 + b])
                    op.then_inc(small_out, 1)
                else:
                    act.activation(SM[par][:, :, :], PS[par][:, :, T:2 * T], ACT.Copy).then_inc(small_out, 1)

            act.wait_ge(gain_out, 1)
            for c in range(CD):
                for k in range(KC * c, KC * (c + 1)):
                    act.wait_ge(x_turned, k + 1)
                    act.activation(U[:, k, 0:T], XB[k % len(XB)], ACT.Copy, scale=NW[:, k:k + 1]).then_inc(u_hi, 1)
                hi(c // RING, c % RING, free=c >= RING)
                act.wait_ge(x_loaded[c], 16)
                act.drain()
                act.activation(SQA[:, :], XS[:, 0, c * XW:(c + 1) * XW], ACT.Square,
                               accum_out=SSQ[:, 0, c:c + 1]).then_inc(x_sq, 1)
            def attention(a, slot):
                if slot == 1:
                    act.wait_ge(drained, 4 * a + 4)
                    act.activation(SG[:, :], G[:, :], ACT.Sigmoid).then_inc(gate_g, 1)
                if slot == 11:
                    act.wait_ge(o_done, a + 1)
                    for g in range(4):
                        act.activation(O2[:, g * P:(g + 1) * P], OB[:, g * P:(g + 1) * P], ACT.Square,
                                       accum_out=RS[:, 4, g:g + 1])
                    act.drain()
                    act.activation(RS[:, 0, :], RS[:, 4, :], ACT.Sqrt, bias=EPT[:, :],
                                   scale=1.0 / P).then_inc(std_ready, 1)

            def gates(i):
                for h in range(2):
                    one = bass.ds(i * 2 + h, 1)
                    act.activation(PRE[:, h * T:(h + 1) * T], SF[:, h * T:(h + 1) * T], ACT.Identity,
                                   scale=OMLB[:, one], bias=LB[:, one])
                act.drain()
                act.activation(K[:, :], PRE[:, :], ACT.Copy, scale=-1.0, bias=1.0).then_inc(gate_f, 1)

            def branch(i, turn0, group0, a=None, first=False, is_conv=False):
                for slot in range(SLOTS):
                    for c in (2 * slot, 2 * slot + 1):
                        if not (first and slot < EARLY):
                            hi(turn0 + TURNS_BRANCH * i + c // RING + 1, c % RING)
                    if a is not None:
                        attention(a, slot)
                    if first and slot == 3:
                        act.wait_ge(x_var, 1)
                        act.activation(ST[:, 10:12], ST[:, 8:10], ACT.Sqrt, bias=EPT[:, :], scale=1.0 / D).then_inc(x_std, 1)
                    if first and slot == 6:
                        act.wait_ge(lb_shift, 1)
                        act.activation(LT[:, 0:32], LT[:, 0:32], ACT.Exp).then_inc(lb_exp, 1)
                    if slot == 5:
                        act.wait_ge(drained, group0 + 4 * i + 1)
                        op = act.activation(SF[:, :], F[:, :], ACT.Sigmoid)
                        if is_conv:
                            op.then_inc(gate_f, 1)
                    if slot == 14 and not is_conv:
                        act.drain()
                        if a is None:
                            act.wait_ge(lb_ready, 1)
                        else:
                            act.wait_ge(level_ready, 8 * a + 8)
                        gates(i)
                    if slot % 4 == 3:
                        n = slot // 4
                        small_half(group0 + 4 * i + n, RING * (turn0 + TURNS_BRANCH * i) + CD * (n + 1), n % 2, free=not (first and n < 2), positions=n == 2 and not is_conv)

            branch(0, 0, 0, first=True)
            with act.Fori(1, NP) as i:
                branch(i, 0, 0, a=i - 1)
            branch(0, CONV_TURN, CONV_GROUP, a=NP - 1, is_conv=True)
            with act.Fori(1, NP) as i:
                branch(i, CONV_TURN, CONV_GROUP, is_conv=True)

            def merge(i, last=False):
                turn = MERGE_TURN + TURNS_MERGE * i + 1
                group = MERGE_GROUP + 4 * i
                chunks = RING * (MERGE_TURN + TURNS_MERGE * i)
                for c in range(2 * CD + 2 * CB):
                    hi(turn + c // RING, c % RING)
                    if c in (CD + 2, 2 * CD + 2):
                        n = c // CD - 1
                        act.wait_ge(drained, group + n + 1)
                        for t in range(2):
                            gate = (GA, GB)[n][:, t * T:(t + 1) * T]
                            act.activation(gate, gate, ACT.Sigmoid,
                                           bias=VT1[:, bass.ds(i * 2 + (32 + n * KT + t), 1)]).then_inc(merge_gate, 1)
                    if c == CD - 1:
                        small_half(group, chunks + c + 1, 0)
                    if c == 2 * CD - 1:
                        small_half(group + 1, chunks + c + 1, 1)
                    if last and c > 2 * CD:
                        split_merged(c - 2 * CD - 1)
                    if c == 2 * CD + CB - 1:
                        small_half(group + 2, chunks + c + 1, 0)
                    if c == 2 * CD + 2 * CB - 1:
                        small_half(group + 3, chunks + c + 1, 1)

            def split_merged(n):
                act.wait_ge(w_used, RING * OUT_TURN - 2 * CB)
                act.wait_ge(merged, 2 * n + 2)
                act.activation(U[:, KC * n:KC * (n + 1), 0:T], MRG[:, KC * n:KC * (n + 1), :], ACT.Copy).then_inc(m_hi, 1)

            with act.Fori(0, NG - 1) as i:
                merge(i)
            merge(NG - 1, last=True)
            split_merged(CD - 1)

            def output(i, last=False):
                for n in range(2):
                    for c in range(CD if not (last and n == 1) else RING):
                        hi(OUT_TURN + TURNS_OUT * i + (n * CD + c) // RING + 1, c % RING)
                    if last and n == 1:
                        act.activation(ST[:, 19:20], EPT[:, :], ACT.Sqrt)
                        break
                    small_half(OUT_GROUP + 2 * i + n, RING * (OUT_TURN + TURNS_OUT * i) + CD * (n + 1), n)
                    act.wait_ge(h_ready, 2 * i + n + 1)
                    for b in range(2):
                        act.activation(SM[n][:, b, :], (GA, GB)[n][:, b * T:(b + 1) * T], ACT.Square,
                                       accum_out=SSQ[:, b, bass.ds(i * 2 + n, 1)]).then_inc(h_sq, 1)

            with act.Fori(0, NG // 2 - 1) as i:
                output(i)
            output(NG // 2 - 1, last=True)
            for b in range(2):
                act.wait_ge(tail_var, b + 1)
                act.activation(ST[:, 10 + b:11 + b], ST[:, 8 + b:9 + b], ACT.Sqrt, bias=EPT[:, :],
                               scale=1.0 / D).then_inc(tail_std, 1)
                act.wait_ge(tail_rstd, b + 1)
                for half, c, done, _ in OUT_PIECES:
                    if half == b and done is out_act:
                        piece = H[:, b, c * XC:(c + 1) * XC]
                        act.activation(piece, piece, ACT.Copy, scale=ST[:, 12 + b:13 + b]).then_inc(out_act, 1)

        @block.vector
        def _(dve):
            channels, positions = "1/rms in the free axis", "1/rms on the partitions"

            def after():
                dve.drain()

            def rstd(r, std, var, tmp):
                dve.reciprocal(r, std)
                after()
                dve.tensor_tensor(tmp, r, r, ALU.mult)
                after()
                dve.tensor_tensor(tmp, tmp, var, ALU.mult)
                after()
                dve.tensor_scalar(tmp, tmp, -0.5, 1.5, ALU.mult, ALU.add)
                after()
                return dve.tensor_tensor(r, r, tmp, ALU.mult)

            dve.wait_ge(gain_turned, 1)
            dve.tensor_copy(NW[:, :], PS[0][:, 0, 0:KT]).then_inc(gain_out, 1)
            after()

            def lo(turn, s):
                dve.wait_ge(hi_ready, RING * turn + s + 1)
                dve.tensor_tensor(WS[s][:, :, GW:2 * GW], RAW[s][:, :, :], WS[s][:, :, 0:GW],
                                  ALU.subtract).then_inc(lo_ready, 1)

            for c in range(CD):
                for k in range(KC * c, KC * (c + 1)):
                    dve.wait_ge(u_hi, k + 1)
                    dve.scalar_tensor_tensor(U[:, k, T:2 * T], XB[k % len(XB)], NW[:, k:k + 1], U[:, k, 0:T],
                                             ALU.mult, ALU.subtract).then_inc(u_ready, 1)
                lo(c // RING, c % RING)
                piece = XS[:, 1, c * XW:(c + 1) * XW]
                dve.wait_ge(x_loaded[c], 16)
                dve.tensor_tensor_reduce(out=SQD[:, :], in0=piece, in1=piece, scale=1.0, scalar=0.0,
                                         op0=ALU.mult, op1=ALU.add, accum_out=SSQ[:, 1, c:c + 1])
                after()
            def x_rms():
                dve.wait_ge(x_sq, CD)
                dve.tensor_reduce(ST[:, 8:10], SSQ[:, :, 0:CD], AX.X, ALU.add).then_inc(x_var, 1)
                after()
                dve.tensor_scalar(ST[:, 14:16], ST[:, 8:10], 1.0 / D, EPS, ALU.mult, ALU.add)
                dve.wait_ge(x_std, 1)
                after()
                rstd(ST[:, 12:14], ST[:, 10:12], ST[:, 14:16], ST[:, 16:18])
                after()
                for b in range(2):
                    op = dve.tensor_scalar(GA[:, b * P:(b + 1) * P], IDN[:, :], ST[:, 12 + b:13 + b], None, ALU.mult)
                op.then_inc(x_rstd, 1)

            def lower_bounds():
                dve.wait_ge(vec_turned, 1)
                dve.tensor_copy(VT1[:, :], SC[1][:, 0:96])
                dve.tensor_copy(VT2[:, :], SC[1][:, 96:145])
                after()
                dve.tensor_tensor(LT[:, 32:48], VT1[:, 0:16], VT1[:, 16:32], ALU.max)
                after()
                dve.tensor_tensor(LT[:, 0:16], VT1[:, 0:16], LT[:, 32:48], ALU.subtract)
                dve.tensor_tensor(LT[:, 16:32], VT1[:, 16:32], LT[:, 32:48], ALU.subtract).then_inc(lb_shift, 1)
                dve.wait_ge(consts, N_CONSTS)
                dve.wait_ge(lb_exp, 1)
                dve.tensor_tensor(LT[:, 32:48], LT[:, 0:16], LT[:, 16:32], ALU.add)
                after()
                dve.reciprocal(LT[:, 32:48], LT[:, 32:48])
                after()
                dve.tensor_tensor(LB[:, :], LT[:, 0:16], LT[:, 32:48], ALU.mult)
                after()
                dve.tensor_scalar(OMLB[:, :], LB[:, :], -1.0, 1.0, ALU.mult, ALU.add).then_inc(lb_ready, 1)

            def drain_group(dst, group, par, norm=None):
                big, small = PS[par][:, :, 0:T], SM[par][:, :, :]
                if dst.shape[1] == 4:
                    dst = dst.rearrange("p (t h) x -> p t h x", t=2)
                    big, small = [v.rearrange("p t (h x) -> p t h x", h=2) for v in (big, small)]
                dve.wait_ge(small_out, group + 1)
                if norm is positions:
                    for b in range(2):
                        op = dve.scalar_tensor_tensor(dst[:, b, :], big[:, b, :], ST[:, 12 + b:13 + b],
                                                      small[:, b, :], ALU.mult, ALU.add)
                elif norm is channels:
                    dve.tensor_tensor(small, big, small, ALU.add)
                    after()
                    factor = RB[:, :].unsqueeze(1).broadcast_to([P, 2, T])
                    if len(small.shape) == 4:
                        factor = factor.rearrange("p t (h x) -> p t h x", h=2)
                    op = dve.tensor_tensor(dst, small, factor, ALU.mult)
                else:
                    op = dve.tensor_tensor(dst, big, small, ALU.add)
                op.then_inc(drained, 1)

            def pair(t):
                return t[:, :].rearrange("p (t n) -> p t n", t=2)

            def store_y(y, kt):
                ys = Y[:, bass.ds(kt, 2), :]
                dve.tensor_copy(ys[:, :, 0:T], y)
                after()
                dve.tensor_tensor(ys[:, :, T:2 * T], y, ys[:, :, 0:T], ALU.subtract).then_inc(y_ready, 1)

            def halves(t, m):
                v = t.rearrange("p (n two m) -> p n two m", two=2, m=m)
                return v[:, :, 0, :], v[:, :, 1, :]

            def produce(n):
                m = LEVELS[n]
                blocks = W2 // (2 * m)
                p_left, p_right = halves(PRE[:, :], m)
                s_left, s_right = halves(SUF[:, :], m)
                if m < P:
                    q_right = QX[:, :, 0:P].rearrange("p g (n two m) -> p g n two m", two=2, m=m)[:, :, :, 1, :]
                    qr = QX[:, :, P:] if m == 1 else QR[:, n % 2, :].rearrange("p (g n) -> p g n", g=4)
                    qr = qr.rearrange("p g (n m) -> p g n m", m=m)
                    op = dve.tensor_tensor(qr, q_right, p_right.rearrange("p (g n) m -> p g n m", g=4), ALU.mult)
                else:
                    q_right = QX[:, :, 0:P].rearrange("p (h two) x -> p h two x", two=2)[:, :, 1, :]
                    qr = QR[:, n % 2, :].rearrange("p (h x) -> p h x", h=2)
                    op = dve.tensor_tensor(qr, q_right, p_right, ALU.mult)
                if m > 1:
                    op = dve.tensor_tensor(halves(KL[:, n % 2, :], m)[0], halves(K[:, :], m)[0], s_left, ALU.mult)
                op.then_inc(level_ready, 1)
                if m == T // 2:
                    return
                over_right = p_right[:, :, m - 1:m].broadcast_to([P, blocks, m])
                over_left = p_left[:, :, m - 1:m].broadcast_to([P, blocks, m])
                if m == 1:
                    dve.memset(s_right, 1.0)
                    dve.tensor_copy(s_left, over_right)
                else:
                    dve.tensor_tensor(s_left, s_left, over_right, ALU.mult)
                after()
                dve.tensor_tensor(p_right, p_right, over_left, ALU.mult)
                after()

            def consume(a, n):
                m = LEVELS[n]
                if m == P:
                    dve.tensor_copy(AO[:, :, :], SC[n % 2][:, 0:T].rearrange("p (h t) -> p h t", h=2)).then_inc(level_read, 1)
                    return
                after()
                if m == P // 2:
                    dve.tensor_copy(AD[0:m, :, m:P], SC[n % 2][0:m, 0:T].rearrange("p (g t) -> p g t", g=4)).then_inc(level_read, 1)
                    return
                dst = AD[:, :, :].rearrange("p g (j two r) -> p g j two r", two=2, r=m)[:, :, :, 1, :]
                mask = MASK[:, n * 64:(n + 1) * 64].bitcast(U32).rearrange("p (j r) -> p j r", r=m)
                if n == 0:
                    eye = IDN[:, :].bitcast(U32).unsqueeze(1).broadcast_to([P, 2, P])
                    banks = [b[:, 0:2 * 192].rearrange("p (g t) -> p g t", g=2) for b in (SC[0], SS)]
                    for b in range(2):
                        dve.copy_predicated(AD[:, 2 * b:2 * b + 2, :], eye, banks[b][:, :, 0:P])
                    after()
                    for b in range(2):
                        op = dve.copy_predicated(dst[:, 2 * b:2 * b + 2], mask.unsqueeze(1).broadcast_to([P, 2, 64, 1]),
                                                 banks[b][:, :, P:].unsqueeze(3))
                    op.then_inc(level_read, 1)
                    return
                rows = slice(0, P - m)
                data = SC[n % 2][rows, 0:T].rearrange("p (g j r) -> p g j r", g=4, r=m)
                mask = mask[rows].unsqueeze(1).broadcast_to([P - m, 4, 64 // m, m])
                dve.copy_predicated(dst[rows], mask, data).then_inc(level_read, 1)

            def attention(a, slot):
                if slot == 0:
                    dve.wait_ge(gate_f, a + 1)
                if 2 <= slot < 10:
                    consume(a, slot - 2)
                if slot < 8:
                    produce(slot)
                if slot == 12:
                    dve.wait_ge(std_ready, a + 1)
                    dve.tensor_scalar(RS[:, 1, :], RS[:, 4, :], 1.0 / P, EPS, ALU.mult, ALU.add)
                    after()
                    rstd(RS[:, 2, :], RS[:, 0, :], RS[:, 1, :], RS[:, 3, :])
                    after()
                    dve.tensor_tensor(O[:, :].rearrange("p (g e) -> p g e", g=4),
                                      OB[:, :].rearrange("p (g e) -> p g e", g=4),
                                      RS[:, 2, :].unsqueeze(2).broadcast_to([P, 4, P]), ALU.mult).then_inc(o_ready, 1)
                if slot == 14:
                    dve.wait_ge(gate_g, a + 1)
                    dve.wait_ge(o_turned, a + 1)
                    dve.tensor_scalar(O[:, :], SS[:, :], HW0, None, ALU.mult)
                    dve.tensor_tensor(SG[:, :], SG[:, :], G[:, :], ALU.mult)
                    after()
                    dve.tensor_tensor(O[:, :], O[:, :], SG[:, :], ALU.mult)
                    after()
                    store_y(pair(O), a * 2)

            def conv(i, slot):
                if slot == 8:
                    dve.wait_ge(gate_f, NP + i + 1)
                    dve.tensor_tensor(SF[:, :], SF[:, :], F[:, :], ALU.mult)
                if slot == 12:
                    dve.memset(UP[:, :, 0:2], 0.0)
                    dve.tensor_tensor(UP[:, :, 2:T + 2], pair(QC), pair(V), ALU.mult)
                    after()
                if slot == 13:
                    for j in range(3):
                        for t in range(2):
                            tap = VT2[:, bass.ds(i * 2 + (16 * j + t), 1)]
                            acc = K[:, t * T:(t + 1) * T]
                            if j == 0:
                                dve.tensor_scalar(acc, UP[:, t, j:T + j], tap, None, ALU.mult)
                            else:
                                dve.scalar_tensor_tensor(acc, UP[:, t, j:T + j], tap, acc, ALU.mult, ALU.add)
                        after()

            def branch(i, turn0, group0, a=None, first=False, is_conv=False):
                for slot in range(SLOTS):
                    for c in (2 * slot, 2 * slot + 1):
                        if a is not None and c == 2 * slot + 1 and 2 <= slot < 10:
                            dve.wait_ge(level_done, 8 * a + slot - 1)
                        if not (first and slot < EARLY):
                            lo(turn0 + TURNS_BRANCH * i + c // RING + 1, c % RING)
                    if first and slot == 6:
                        lower_bounds()
                    if a is not None:
                        attention(a, slot)
                    if is_conv:
                        conv(i, slot)
                    if slot % 4 == 3:
                        n = slot // 4
                        after()
                        if n == 2 and a is not None:
                            dve.wait_ge(o_done, a + 1)
                        if first and n == 0:
                            x_rms()
                            dve.wait_ge(x_spread, 1)
                            dve.tensor_copy(RB[:, :], SC[0][:, 0:T])
                            after()
                        q = pair(QC) if is_conv else QX[:, :, 0:P]
                        drain_group((pair(F), q, pair(V), pair(G))[n], group0 + 4 * i + n, n % 2,
                                    norm=positions if n == 2 and not is_conv else channels)
                        after()
                if is_conv:
                    dve.tensor_tensor(K[:, :], K[:, :], G[:, :], ALU.mult)
                    after()
                    dve.tensor_tensor(K[:, :], K[:, :], SF[:, :], ALU.mult)
                    after()
                    store_y(pair(K), i * 2 + KB)
                    after()

            branch(0, 0, 0, first=True)
            with dve.Fori(1, NP) as i:
                branch(i, 0, 0, a=i - 1)
            branch(0, CONV_TURN, CONV_GROUP, a=NP - 1, is_conv=True)
            with dve.Fori(1, NP) as i:
                branch(i, CONV_TURN, CONV_GROUP, is_conv=True)

            def split_merged(n):
                dve.wait_ge(m_hi, n + 1)
                k = slice(KC * n, KC * (n + 1))
                dve.tensor_tensor(U[:, k, T:2 * T], MRG[:, k, :], U[:, k, 0:T], ALU.subtract).then_inc(m_ready, 1)

            def merge(i, last=False):
                turn = MERGE_TURN + TURNS_MERGE * i + 1
                group = MERGE_GROUP + 4 * i
                out2 = MRG[:, bass.ds(i * 2, 2), :]
                for c in range(2 * CD + 2 * CB):
                    lo(turn + c // RING, c % RING)
                    if c == CD - 1:
                        drain_group(pair(GA), group, 0, norm=channels)
                    if c == 2 * CD - 1:
                        drain_group(pair(GB), group + 1, 1, norm=channels)
                    if last and c > 2 * CD:
                        split_merged(c - 2 * CD - 1)
                    if c == 2 * CD + CB - 1:
                        drain_group(pair(Z), group + 2, 0)
                        after()
                        dve.wait_ge(merge_gate, 4 * i + 2)
                        dve.tensor_tensor(out2, pair(GA), pair(Z), ALU.mult)
                        after()
                drain_group(pair(Z), group + 3, 1)
                after()
                dve.wait_ge(merge_gate, 4 * i + 4)
                dve.tensor_tensor(Z[:, :], GB[:, :], Z[:, :], ALU.mult)
                after()
                dve.tensor_tensor(out2, out2, pair(Z), ALU.add).then_inc(merged, 1)
                after()

            with dve.Fori(0, NG - 1) as i:
                merge(i)
            merge(NG - 1, last=True)
            split_merged(CD - 1)

            def output(i, first=False, last=False):
                for n in range(2):
                    for c in range(CD if not (last and n == 1) else RING):
                        lo(OUT_TURN + TURNS_OUT * i + (n * CD + c) // RING + 1, c % RING)
                    if last and n == 1:
                        break
                    h = pair((GA, GB)[n])
                    if not first:
                        dve.wait_ge(h_sq, 4 * i + 2 * n - 2)
                    drain_group(h, OUT_GROUP + 2 * i + n, n)
                    after()
                    cols = bass.ds(i * 2 * GW + n * GW, GW)
                    dve.wait_ge(xr_loaded[n], i * 32 + 32)
                    dve.tensor_tensor(h, h, XR[:, :, cols], ALU.add).then_inc(h_ready, 1)
                    after()
                    fw = FW[:, cols].unsqueeze(1).broadcast_to([P, 2, GW])
                    dve.tensor_tensor(H[:, :, cols], h, fw, ALU.mult)

            output(0, first=True)
            with dve.Fori(1, NG // 2 - 1) as i:
                output(i)
            output(NG // 2 - 1, last=True)
            dve.wait_ge(h_sq, 2 * NG - 2)
            dve.wait_ge(xr_loaded[1], NG // 2 * 32)
            cols = slice(D - GW, D)
            for b in range(2):
                h, small = GB[:, b * T:(b + 1) * T], SM[1][:, b, :]
                dve.wait_ge(half_summed, b + 1)
                dve.tensor_tensor(small, PS[1][:, b, T:2 * T], XR[:, b, cols], ALU.add)
                after()
                dve.tensor_tensor(h, PS[1][:, b, 0:T], small, ALU.add)
                after()
                dve.tensor_tensor_reduce(out=small, in0=h, in1=h, scale=1.0, scalar=0.0, op0=ALU.mult,
                                         op1=ALU.add, accum_out=SSQ[:, b, NG - 1:NG])
                after()
                dve.tensor_reduce(ST[:, 8 + b:9 + b], SSQ[:, b, :], AX.X, ALU.add).then_inc(tail_var, 1)
                dve.tensor_tensor(H[:, b, cols], h, FW[:, cols], ALU.mult)
                after()
                dve.tensor_scalar(ST[:, 14 + b:15 + b], ST[:, 8 + b:9 + b], 1.0 / D, EPS, ALU.mult, ALU.add)
                dve.wait_ge(tail_std, b + 1)
                after()
                rstd(*[ST[:, c + b:c + b + 1] for c in (12, 10, 14, 16)]).then_inc(tail_rstd, 1)
                after()
                for half, c, done, _ in OUT_PIECES:
                    if half == b and done is out_dve:
                        piece = H[:, b, c * XC:(c + 1) * XC]
                        dve.tensor_scalar(piece, piece, ST[:, 12 + b:13 + b], None, ALU.mult).then_inc(out_dve, 1)

        @block.tensor
        def _(pe):
            pe.wait_ge(consts, IDN_WRITTEN)
            pe.wait_ge(gain_loaded, 16)
            pe.transpose(PS[0][:, 0, 0:KT], VEC0[:, :], IDN[0:KT, 0:KT]).then_inc(gain_turned, 1)

            def turn_x(k):
                if k % KC == 0:
                    pe.wait_ge(x_loaded[k // KC], 16)
                if k >= len(XB):
                    pe.wait_ge(u_ready, k - len(XB) + 1)
                for b in range(2):
                    op = pe.transpose(XB[k % len(XB)][:, b * P:(b + 1) * P], XS[:, b, k * P:(k + 1) * P], IDN[:, :])
                op.then_inc(x_turned, 1)

            for k in range(KC):
                turn_x(k)

            def split_product(bank, stat_hi, stat_lo, both, first, last):
                def with_lo(stop):
                    return pe.matmul(bank[:, T:2 * T], stat_lo, both[:, 0:T], start=False, stop=stop,
                                     skip_group_check=True)

                if not first:
                    with_lo(False)
                op = pe.matmul(bank, stat_hi, both, start=first, stop=last, skip_group_check=True)
                return with_lo(False) if first else op

            def channels(par, s, rhs, k0, n_tiles):
                for k in range(KC):
                    for t in range(2):
                        op = split_product(PS[par][:, t, :], WS[s][:, k, t * P:(t + 1) * P],
                                           WS[s][:, k, GW + t * P:GW + (t + 1) * P], rhs[:, k0 + k, :],
                                           k0 + k == 0, k0 + k == n_tiles - 1)
                return op

            def positions(par, s, lhs, k0, n_tiles, halves=(0, 1)):
                for k in range(KC):
                    for b in halves:
                        op = split_product(PS[par][:, b, :], lhs[:, k0 + k, b * P:(b + 1) * P],
                                           lhs[:, k0 + k, T + b * P:T + (b + 1) * P], WS[s][:, k, :],
                                           k0 + k == 0, k0 + k == n_tiles - 1)
                return op

            def attention(a, c):
                if c % 2 == 0 and 4 <= c < 20:
                    n = (c - 4) // 2
                    pe.wait_ge(level_ready, 8 * a + (n + 1))
                    if n >= 2:
                        pe.wait_ge(level_read, 8 * a + (n - 1))
                    if n == 7:
                        for h in range(2):
                            op = pe.matmul(SC[n % 2][:, h * P:(h + 1) * P], KL[:, n % 2, h * T:h * T + P],
                                           QR[:, n % 2, h * P:(h + 1) * P], start=True, stop=True)
                    else:
                        for g in range(4):
                            out = SC[n % 2][0:P - LEVELS[n], g * 64:(g + 1) * 64]
                            k_side = KL[:, n % 2, g * P:(g + 1) * P - LEVELS[n]]
                            q_side = QR[:, n % 2, g * 64:(g + 1) * 64]
                            if n == 0:
                                out = (SC[0], SS)[g // 2][:, g % 2 * 192:(g % 2 + 1) * 192]
                                k_side, q_side = K[:, g * P:(g + 1) * P], QX[:, g, :]
                            op = pe.matmul(out, k_side, q_side, start=True, stop=True)
                    op.then_inc(level_done, 1)
                if c == 22:
                    pe.wait_ge(level_read, 8 * a + 8)
                    for h in range(2):
                        v = [V[:, b * T + h * P:b * T + (h + 1) * P] for b in range(2)]
                        o = [OB[:, h * T + b * P:h * T + (b + 1) * P] for b in range(2)]
                        pe.matmul(o[0], AD[:, 2 * h, :], v[0], start=True, stop=True)
                        pe.matmul(o[1], AO[:, h, :], v[0], start=True, stop=False)
                        op = pe.matmul(o[1], AD[:, 2 * h + 1, :], v[1], start=False, stop=True)
                    op.then_inc(o_done, 1)
                if c == 27:
                    pe.wait_ge(o_ready, a + 1)
                    for g in range(4):
                        op = pe.transpose(SS[:, g * P:(g + 1) * P], O[:, g * P:(g + 1) * P], IDN[:, :])
                    op.then_inc(o_turned, 1)

            def group(turn, n0, n_chunks, mode, operand, k_start, par, gidx, free=True, u_wait=None, a=None):
                if free:
                    pe.wait_ge(drained, gidx - 1)
                for c in range(n_chunks):
                    if u_wait is not None and u_wait[0] is u_ready:
                        for k in range(KC * (c + 1), min(KC * (c + 2), KT)):
                            turn_x(k)
                    if u_wait is not None:
                        pe.wait_ge(u_wait[0], u_wait[1] * (c + 1))
                    at_chunk = n0 + c
                    pe.wait_ge(lo_ready, RING * (turn + at_chunk // RING) + at_chunk % RING + 1)
                    op = mode(par, at_chunk % RING, operand[:, k_start:k_start + n_chunks * KC, :], c * KC,
                              n_chunks * KC)
                    op.then_inc(w_used, 1)
                    if a is not None:
                        attention(a, at_chunk)
                    if u_wait is None and not free and c == 1:
                        pe.wait_ge(vec_loaded, 64)
                        pe.transpose(SC[1][:, 0:96], VEC1[0:96, :], IDN[0:96, 0:96])
                        pe.transpose(SC[1][:, 96:145], VEC2[0:49, :], IDN[0:49, 0:49]).then_inc(vec_turned, 1)
                        pe.wait_ge(consts, N_CONSTS)
                        pe.wait_ge(x_rstd, 1)
                        pe.matmul(SC[0][:, 0:T], ONES[:, :], GA[:, 0:T], start=True, stop=True).then_inc(x_spread, 1)

            def branch(i, turn0, group0, modes, a=None, first=False):
                for n in range(4):
                    group(turn0 + TURNS_BRANCH * i, n * CD, CD, modes[n], U, 0, n % 2, group0 + 4 * i + n,
                          free=not (first and n < 2), u_wait=(u_ready, KC) if first and n == 0 else None, a=a)

            hgrn = (channels, channels, positions, channels)
            branch(0, 0, 0, hgrn, first=True)
            with pe.Fori(1, NP) as i:
                branch(i, 0, 0, hgrn, a=i - 1)
            branch(0, CONV_TURN, CONV_GROUP, (channels,) * 4, a=NP - 1)
            with pe.Fori(1, NP) as i:
                branch(i, CONV_TURN, CONV_GROUP, (channels,) * 4)
            with pe.Fori(0, NG) as i:
                turn, g = MERGE_TURN + TURNS_MERGE * i, MERGE_GROUP + 4 * i
                group(turn, 0, CD, channels, U, 0, 0, g)
                group(turn, CD, CD, channels, U, 0, 1, g + 1)
                pe.wait_ge(y_ready, 2 * NP)
                group(turn, 2 * CD, CB, channels, Y, 0, 0, g + 2)
                group(turn, 2 * CD + CB, CB, channels, Y, KB, 1, g + 3)

            def output(i, first=False, last=False):
                for n in range(1 if last else 2):
                    group(OUT_TURN + TURNS_OUT * i, n * CD, CD, positions, U, 0, n, OUT_GROUP + 2 * i + n,
                          u_wait=(m_ready, 1) if first and n == 0 else None)

            output(0, first=True)
            with pe.Fori(1, NG // 2 - 1) as i:
                output(i)
            output(NG // 2 - 1, last=True)
            turn = OUT_TURN + TURNS_OUT * (NG // 2) - CD // RING
            pe.wait_ge(drained, OUT_GROUP + NG - 2)
            for b in range(2):
                for c in range(CD):
                    if b == 0:
                        pe.wait_ge(lo_ready, RING * turn + c + 1)
                    if b == 0 or c >= CD - RING:
                        op = positions(1, c % RING, U, c * KC, KT, (0, 1) if c < CD - RING else (b,))
                    if c < CD - RING and b == 0:
                        op.then_inc(w_used, 1)
                op.then_inc(half_summed, 1)


_INS = ["x", "norm_w", "w_in", "lb_logits", "hgrn_norm_w", "conv_w", "w_branch_a", "w_branch_b",
        "gate_bias", "w_out", "final_norm_w"]


def kernel(**inputs):
    import numpy as np
    import concourse.bacc as bacc
    from concourse import mybir as mb
    from concourse.bass_utils import run_bass_kernel_spmd

    nc = bacc.Bacc("TRN2", target_bir_lowering=False, num_devices=1, dynamic_dma_scratch_size=1024)
    arrays, args = {}, []
    for name in _INS:
        a = np.ascontiguousarray(inputs[name])
        arrays[f"in_{name}"] = a
        args.append(nc.dram_tensor(f"in_{name}", a.shape, mb.dt.from_np(a.dtype), kind="ExternalInput").ap())
    out = nc.dram_tensor("out_dram", (1, T, D), F32, kind="ExternalOutput").ap()
    build(nc, *args, out)
    r = run_bass_kernel_spmd(nc, [arrays], core_ids=[0])
    return r.results[0]["out_dram"]
```
